# Optimizing a Trainium2 kernel written in Bass

```python
import jax
import jax.numpy as jnp
from jax import lax
import numpy as np

D_MODEL = 1024
BATCH = 1
SEQ = 256
DEPTH = 2

GRID_W = 64
CTX_LEN = 256
MLA_HEADS = 8
MLA_NOPE = 64
MLA_ROPE = 32
MLA_V = 64
MLA_Q_LORA = 256
MLA_KV_LORA = 128
MLA_SCALE = (MLA_NOPE + MLA_ROPE) ** -0.5
NA_HEADS = 4
NA_HEAD_DIM = 64
NA_WIN_R = 8
NA_WIN_C = 16
NA_COL_BLOCK = 16
NA_KEY_COLS = 32
NA_SCALE = NA_HEAD_DIM ** -0.5
FT_GROUPS = 4
FT_GROUP_DIM = 64
N_EXPERTS = 16
N_GROUPS = 4
EXPERTS_PER_GROUP = N_EXPERTS // N_GROUPS
TOP_K = 2
EXPERT_FF = 256

ROPE_THETA = 10000.0
NORM_EPS = 1e-6
Q_BLOCK = 128
NEG_INF = -1e30
N_BRANCH = 3
MLA_WIDTH = MLA_HEADS * MLA_V
NA_WIDTH = NA_HEADS * NA_HEAD_DIM
FT_WIDTH = FT_GROUPS * FT_GROUP_DIM
IN_SPLITS = (MLA_Q_LORA, MLA_KV_LORA, MLA_ROPE, NA_WIDTH, NA_WIDTH, NA_WIDTH, FT_WIDTH)
IN_WIDTH = sum(IN_SPLITS)

kernel_name = 'hybrid_mla_natten_fnet_groupmoe_block'

def rmsnorm(x, g):
    xf = x.astype(jnp.float32)
    y = xf * lax.rsqrt(jnp.mean(xf * xf, axis=-1, keepdims=True) + NORM_EPS)
    return (y * g.astype(jnp.float32)).astype(x.dtype)

def split_cols(a, sizes):
    return jnp.split(a, [int(o) for o in np.cumsum(sizes)[:-1]], axis=-1)

def axial_rope_tables(n_tok):
    n_freq = MLA_ROPE // 4
    inv_freq = ROPE_THETA ** (-jnp.arange(n_freq, dtype=jnp.float32) / n_freq)
    t = jnp.arange(n_tok, dtype=jnp.int32)
    row = (t // GRID_W).astype(jnp.float32)
    col = (t % GRID_W).astype(jnp.float32)
    ang = jnp.concatenate([row[:, None] * inv_freq, col[:, None] * inv_freq], axis=-1)
    return jnp.cos(ang), jnp.sin(ang)

def apply_rope(x, cos, sin):
    xf = x.astype(jnp.float32)
    half = xf.shape[-1] // 2
    x1, x2 = xf[..., :half], xf[..., half:]
    return jnp.concatenate([x1 * cos - x2 * sin, x2 * cos + x1 * sin], axis=-1).astype(x.dtype)

def dense_block_attention(q, k, v, scale):
    b, nq, h, dk = q.shape
    dv = v.shape[-1]
    nb = nq // Q_BLOCK
    qb = q.reshape(b, nb, Q_BLOCK, h, dk).transpose(1, 0, 2, 3, 4)

    def one_block(qblk):
        s = jnp.einsum('bqhd,bkhd->bhqk', qblk, k, preferred_element_type=jnp.float32) * scale
        p = jax.nn.softmax(s, axis=-1).astype(v.dtype)
        return jnp.einsum('bhqk,bkhd->bqhd', p, v)

    o = lax.map(one_block, qb)
    return o.transpose(1, 0, 2, 3, 4).reshape(b, nq, h, dv)

def mla_q(q_lat, q_norm_g, w_q_up, cos, sin):
    b, n, _ = q_lat.shape
    q = (rmsnorm(q_lat, q_norm_g) @ w_q_up).reshape(b, n, MLA_HEADS, MLA_NOPE + MLA_ROPE)
    if cos is None:
        return q
    q_nope, q_pe = q[..., :MLA_NOPE], q[..., MLA_NOPE:]
    return jnp.concatenate([q_nope, apply_rope(q_pe, cos[:, None, :], sin[:, None, :])], axis=-1)

def mla_kv(kv_lat, k_rope, kv_norm_g, w_kv_up, cos, sin):
    b, n, _ = kv_lat.shape
    kv = (rmsnorm(kv_lat, kv_norm_g) @ w_kv_up).reshape(b, n, MLA_HEADS, MLA_NOPE + MLA_V)
    k_nope, v = kv[..., :MLA_NOPE], kv[..., MLA_NOPE:]
    if cos is not None:
        k_rope = apply_rope(k_rope, cos, sin)
    k_pe = jnp.broadcast_to(k_rope[:, :, None, :], (b, n, MLA_HEADS, MLA_ROPE))
    return jnp.concatenate([k_nope, k_pe], axis=-1), v

def neighborhood_attention(q, k, v, k_ctx, v_ctx, rpb):
    b, s, hn, d = q.shape
    rows = s // GRID_W
    wr = min(NA_WIN_R, rows)
    n_cb = GRID_W // NA_COL_BLOCK
    r = jnp.arange(rows)
    row_idx = jnp.clip(r - wr // 2, 0, rows - wr)[:, None] + jnp.arange(wr)
    cb = jnp.arange(n_cb)
    col_idx = jnp.clip(cb * NA_COL_BLOCK - NA_WIN_C // 2, 0, GRID_W - NA_KEY_COLS)[:, None] + jnp.arange(NA_KEY_COLS)
    qcol = cb[:, None] * NA_COL_BLOCK + jnp.arange(NA_COL_BLOCK)
    win_start = jnp.clip(qcol - NA_WIN_C // 2, 0, GRID_W - NA_WIN_C)
    col_mask = (col_idx[:, None, :] >= win_start[..., None]) & (col_idx[:, None, :] < win_start[..., None] + NA_WIN_C)
    kg = k.reshape(b, rows, GRID_W, hn, d)[:, row_idx[:, None, :, None], col_idx[None, :, None, :]]
    vg = v.reshape(b, rows, GRID_W, hn, d)[:, row_idx[:, None, :, None], col_idx[None, :, None, :]]
    qg = q.reshape(b, rows, n_cb, NA_COL_BLOCK, hn, d)
    s_loc = jnp.einsum('brcqhd,brcwkhd->brchqwk', qg, kg, preferred_element_type=jnp.float32) * NA_SCALE
    dr_idx = row_idx - r[:, None] + (NA_WIN_R - 1)
    dc_idx = jnp.clip(col_idx[:, None, :] - qcol[:, :, None], -(NA_WIN_C - 1), NA_WIN_C - 1) + (NA_WIN_C - 1)
    bias = rpb.astype(jnp.float32)[:, dr_idx[:, None, None, :, None], dc_idx[None, :, :, None, :]]
    bias = jnp.transpose(bias, (1, 2, 0, 3, 4, 5))
    s_loc = jnp.where(col_mask[None, None, :, None, :, None, :], s_loc + bias[None], NEG_INF)
    s_loc = s_loc.reshape(b, rows, n_cb, hn, NA_COL_BLOCK, wr * NA_KEY_COLS)
    s_ctx = jnp.einsum('brcqhd,bkhd->brchqk', qg, k_ctx, preferred_element_type=jnp.float32) * NA_SCALE
    p = jax.nn.softmax(jnp.concatenate([s_loc, s_ctx], axis=-1), axis=-1).astype(v.dtype)
    n_loc = wr * NA_KEY_COLS
    p_loc = p[..., :n_loc].reshape(b, rows, n_cb, hn, NA_COL_BLOCK, wr, NA_KEY_COLS)
    p_ctx = p[..., n_loc:]
    o = jnp.einsum('brchqwk,brcwkhd->brcqhd', p_loc, vg) + jnp.einsum('brchqk,bkhd->brcqhd', p_ctx, v_ctx)
    return o.reshape(b, s, hn, d)

def fourier_mix(u):
    b, n, _ = u.shape
    ug = u.reshape(b, n, FT_GROUPS, FT_GROUP_DIM).astype(jnp.float32)
    f = jnp.fft.fft2(ug, axes=(1, 3), norm='ortho').real
    return f.reshape(b, n, FT_WIDTH).astype(u.dtype)

def merge_branches(h, o_a, o_b, o_c, w_gate, b_gate, w_br_mla, w_br_na, w_br_ft, w_out):
    g = jax.nn.sigmoid(h @ w_gate + b_gate)
    g_a, g_b, g_c = jnp.split(g, N_BRANCH, axis=-1)
    m = g_a * (o_a @ w_br_mla) + g_b * (o_b @ w_br_na) + g_c * (o_c @ w_br_ft)
    return m @ w_out

def to_heads(t):
    return t.reshape(t.shape[0], t.shape[1], NA_HEADS, NA_HEAD_DIM)

def token_mixers(h_lat, h_ctx, cos, sin, w_in, q_norm_g, w_q_up, kv_norm_g, w_kv_up, rpb,
                 w_gate, b_gate, w_br_mla, w_br_na, w_br_ft, w_out, need_ctx):
    b, s, _ = h_lat.shape
    pl = split_cols(h_lat @ w_in, IN_SPLITS)
    pc = split_cols(h_ctx @ w_in, IN_SPLITS)
    q_l = mla_q(pl[0], q_norm_g, w_q_up, cos, sin)
    k_l, v_l = mla_kv(pl[1], pl[2], kv_norm_g, w_kv_up, cos, sin)
    k_c, v_c = mla_kv(pc[1], pc[2], kv_norm_g, w_kv_up, None, None)
    o_a = dense_block_attention(q_l, jnp.concatenate([k_l, k_c], axis=1),
                                jnp.concatenate([v_l, v_c], axis=1), MLA_SCALE).reshape(b, s, MLA_WIDTH)
    na_kc, na_vc = to_heads(pc[4]), to_heads(pc[5])
    o_b = neighborhood_attention(to_heads(pl[3]), to_heads(pl[4]), to_heads(pl[5]), na_kc, na_vc, rpb).reshape(b, s, NA_WIDTH)
    o_c = fourier_mix(pl[6])
    y_lat = merge_branches(h_lat, o_a, o_b, o_c, w_gate, b_gate, w_br_mla, w_br_na, w_br_ft, w_out)
    if not need_ctx:
        return y_lat, None
    n_c = h_ctx.shape[1]
    q_c = mla_q(pc[0], q_norm_g, w_q_up, None, None)
    oc_a = dense_block_attention(q_c, k_c, v_c, MLA_SCALE).reshape(b, n_c, MLA_WIDTH)
    oc_b = dense_block_attention(to_heads(pc[3]), na_kc, na_vc, NA_SCALE).reshape(b, n_c, NA_WIDTH)
    oc_c = fourier_mix(pc[6])
    y_ctx = merge_branches(h_ctx, oc_a, oc_b, oc_c, w_gate, b_gate, w_br_mla, w_br_na, w_br_ft, w_out)
    return y_lat, y_ctx

def grouped_moe(h, router_w, router_bias, w_g, w_u, w_d):
    b, n, _ = h.shape
    scores = jax.nn.sigmoid(jnp.einsum('bnd,de->bne', h, router_w, preferred_element_type=jnp.float32))
    sel = scores + router_bias.astype(jnp.float32)
    grp_score = lax.top_k(sel.reshape(b, n, N_GROUPS, EXPERTS_PER_GROUP), TOP_K)[0].sum(-1)
    grp_mask = jax.nn.one_hot(jnp.argmax(grp_score, axis=-1), N_GROUPS, dtype=jnp.bool_)
    exp_mask = jnp.repeat(grp_mask, EXPERTS_PER_GROUP, axis=-1)
    _, top_idx = lax.top_k(jnp.where(exp_mask, sel, -jnp.inf), TOP_K)
    top_w = jnp.take_along_axis(scores, top_idx, axis=-1)
    top_w = top_w / jnp.sum(top_w, axis=-1, keepdims=True)
    gate = jnp.sum(jax.nn.one_hot(top_idx, N_EXPERTS, dtype=jnp.float32) * top_w[..., None], axis=-2)
    hid = jax.nn.silu(jnp.einsum('bnd,edf->bnef', h, w_g)) * jnp.einsum('bnd,edf->bnef', h, w_u)
    hid = hid * gate[..., None].astype(h.dtype)
    return jnp.einsum('bnef,efd->bnd', hid, w_d)

def setup_inputs(seed: int = 0) -> dict:
    key = jax.random.key(seed)
    ks = jax.random.split(key, 32)
    cnt = [0]

    def nrm(shape, scale):
        k = ks[cnt[0]]
        cnt[0] += 1
        return jax.random.normal(k, shape, jnp.float32) * scale

    D = D_MODEL
    L = DEPTH
    return {
        'x': nrm((BATCH, SEQ, D), 1.0),
        'c': nrm((BATCH, D), 1.0),
        'ctx': nrm((BATCH, CTX_LEN, D), 1.0),
        'c_ctx': nrm((D,), 1.0),
        'w_ada': nrm((L, D, 6 * D), 0.5 * D ** -0.5),
        'b_ada': nrm((L, 6 * D), 0.02),
        'norm1_g': 1.0 + nrm((L, D), 0.05),
        'norm2_g': 1.0 + nrm((L, D), 0.05),
        'w_in': nrm((L, D, IN_WIDTH), D ** -0.5),
        'q_norm_g': 1.0 + nrm((L, MLA_Q_LORA), 0.05),
        'w_q_up': nrm((L, MLA_Q_LORA, MLA_HEADS * (MLA_NOPE + MLA_ROPE)), MLA_Q_LORA ** -0.5),
        'kv_norm_g': 1.0 + nrm((L, MLA_KV_LORA), 0.05),
        'w_kv_up': nrm((L, MLA_KV_LORA, MLA_HEADS * (MLA_NOPE + MLA_V)), MLA_KV_LORA ** -0.5),
        'na_rpb': nrm((L, NA_HEADS, 2 * NA_WIN_R - 1, 2 * NA_WIN_C - 1), 0.1),
        'w_gate': nrm((L, D, N_BRANCH * D), D ** -0.5),
        'b_gate': nrm((L, N_BRANCH * D), 0.02),
        'w_br_mla': nrm((L, MLA_WIDTH, D), MLA_WIDTH ** -0.5),
        'w_br_na': nrm((L, NA_WIDTH, D), NA_WIDTH ** -0.5),
        'w_br_ft': nrm((L, FT_WIDTH, D), FT_WIDTH ** -0.5),
        'w_out': nrm((L, D, D), D ** -0.5),
        'router_w': nrm((D, N_EXPERTS), D ** -0.5),
        'router_bias': nrm((N_EXPERTS,), 0.01),
        'w_e_gate': nrm((L, N_EXPERTS, D, EXPERT_FF), D ** -0.5),
        'w_e_up': nrm((L, N_EXPERTS, D, EXPERT_FF), D ** -0.5),
        'w_e_down': nrm((L, N_EXPERTS, EXPERT_FF, D), EXPERT_FF ** -0.5),
        'final_norm_g': 1.0 + nrm((D,), 0.05),
    }

def reference(x, c, ctx, c_ctx, w_ada, b_ada, norm1_g, norm2_g, w_in, q_norm_g, w_q_up, kv_norm_g,
              w_kv_up, na_rpb, w_gate, b_gate, w_br_mla, w_br_na, w_br_ft, w_out, router_w, router_bias,
              w_e_gate, w_e_up, w_e_down, final_norm_g):
    cos, sin = axial_rope_tables(x.shape[1])
    silu_c = jax.nn.silu(c)
    silu_cc = jax.nn.silu(c_ctx)
    x_lat, x_ctx = x, ctx
    for l in range(DEPTH):
        need_ctx = l < DEPTH - 1
        mod = silu_c @ w_ada[l] + b_ada[l]
        mod_c = silu_cc @ w_ada[l] + b_ada[l]
        sh1, sc1, g1, sh2, sc2, g2 = jnp.split(mod[:, None, :], 6, axis=-1)
        csh1, csc1, cg1, csh2, csc2, cg2 = jnp.split(mod_c, 6, axis=-1)
        h_lat = rmsnorm(x_lat, norm1_g[l]) * (1.0 + sc1) + sh1
        h_ctx = rmsnorm(x_ctx, norm1_g[l]) * (1.0 + csc1) + csh1
        y_lat, y_ctx = token_mixers(h_lat, h_ctx, cos, sin, w_in[l], q_norm_g[l], w_q_up[l], kv_norm_g[l],
                                    w_kv_up[l], na_rpb[l], w_gate[l], b_gate[l], w_br_mla[l], w_br_na[l],
                                    w_br_ft[l], w_out[l], need_ctx)
        x_lat = x_lat + g1 * y_lat
        h_lat = rmsnorm(x_lat, norm2_g[l]) * (1.0 + sc2) + sh2
        x_lat = x_lat + g2 * grouped_moe(h_lat, router_w, router_bias, w_e_gate[l], w_e_up[l], w_e_down[l])
        if need_ctx:
            x_ctx = x_ctx + cg1 * y_ctx
            h_ctx = rmsnorm(x_ctx, norm2_g[l]) * (1.0 + csc2) + csh2
            x_ctx = x_ctx + cg2 * grouped_moe(h_ctx, router_w, router_bias, w_e_gate[l], w_e_up[l], w_e_down[l])
    return rmsnorm(x_lat, final_norm_g)


_drawn_inputs = setup_inputs


def setup_inputs(seed=0):
    import zlib

    import numpy as np

    out = dict(_drawn_inputs(seed))
    spreads = {}
    factors = {'q_norm_g': 6.754, 'kv_norm_g': 8.0, 'na_rpb': 8.0, 'b_gate': 5.925}
    for name, (base, spread) in spreads.items():
        noise = np.random.default_rng([zlib.crc32(name.encode()), seed]).standard_normal(out[name].shape)
        drawn = base * np.exp(spread * noise) if base else spread * noise
        out[name] = jnp.asarray(drawn.astype(out[name].dtype))
    for name, factor in factors.items():
        out[name] = (out[name] * factor).astype(out[name].dtype)
    return out
```

```python
from contextlib import ExitStack

import concourse.bass as bass
from concourse import mybir
import numpy as np

F32 = mybir.dt.float32
F32R = mybir.dt.float32r
ALU = mybir.AluOpType
ACT = mybir.ActivationFunctionType
AX = mybir.AxisListType.X

P = 128
D = 1024
KB = D // P
S_LAT = 256
S_CTX = 256
T = S_LAT + S_CTX
DEPTH = 2
GRID_W = 64
HEADS, NOPE, ROPE, VD = 8, 64, 32, 64
Q_LORA, KV_LORA = 256, 128
NA_HEADS, NA_D = 4, 64
WIN_R, WIN_C = 8, 16
FT_G, FT_D = 4, 64
N_EXP, N_GRP = 16, 4
PER_GRP = N_EXP // N_GRP
FF = 256
EPS = 1e-6
NEG = -1e30
MLA_SCALE = (NOPE + ROPE) ** -0.5
NA_SCALE = NA_D ** -0.5
MOD = 6 * KB

CH = 2048
CW = 256
N_ADA = MOD * P // CW
N_IN = 6
N_UP = 2
N_MERGE = D // CW
N_OUT = D // CW
RAW = 3
SPL = 2

V_BADA, V_N1, V_N2, V_BG, V_QG, V_KVG = 0, 48, 56, 64, 88, 90
V_LAYER = 91
V_C = DEPTH * V_LAYER
V_FN = V_C + 2 * KB
V_RB = V_FN + KB
V_RW = V_RB + N_EXP
V_ALL = V_RW + KB * N_EXP


def build(nc, wts, xin, vecs, rope, dft, biases, out, gate_rows):
    ctx = ExitStack()
    with ctx:
        base = nc.sbuf_base + (-nc.sbuf_base) % 64
        at = [base]

        def place(name, shape, dt, off=None):
            size = 4 * int(np.prod(shape[1:]))
            o = at[0] if off is None else off
            if off is None:
                at[0] += size + (-size) % 32
            return nc.alloc_sbuf_tensor_at(name, shape, dt, offset=o)

        x = place("x", [P, KB, T], F32)
        h_hi = place("h_hi", [P, KB, T], F32R)
        h_lo = place("h_lo", [P, KB, T], F32R)
        raw = place("raw", [P, RAW, CH], F32)
        w_hi = place("w_hi", [P, SPL, CH], F32R)
        w_lo = place("w_lo", [P, SPL, CH], F32R)
        sq = place("sq", [P, 2, T], F32)
        rinv = place("rinv", [P, T], F32)
        vec = place("vec", [P, V_ALL], F32)
        ident = place("ident", [P, P], F32)
        ones = place("ones", [P, P], F32)
        eps = place("eps", [P, 1], F32)
        cs = place("cs", [P, KB, 2], F32)
        mod = place("mod", [P, DEPTH, MOD, 2], F32)
        coef = place("coef", [P, DEPTH, 2, KB, 2], F32)
        rw_hi = place("rw_hi", [P, KB, N_EXP], F32R)
        rw_lo = place("rw_lo", [P, KB, N_EXP], F32R)
        smx = place("smx", [P, 4, 8], F32)
        A0 = at[0]
        K1 = 1024
        q = place("q", [P, HEADS, T], F32, A0)
        lat_hi = place("lat_hi", [P, 3, T], F32R, A0 + 16 * K1)
        lat_lo = place("lat_lo", [P, 3, T], F32R, A0 + 22 * K1)
        k = place("k", [P, HEADS, T], F32, A0 + 32 * K1)
        v = place("v", [P, T // P, HEADS * VD], F32, A0 + 48 * K1)
        lat = place("lat", [P, 3, T], F32, A0 + 48 * K1)
        naq = place("naq", [P, 2, T], F32, A0 + 56 * K1)
        nak = place("nak", [P, 2, T], F32, A0 + 60 * K1)
        nav = place("nav", [P, T // P, 256], F32, A0 + 64 * K1)
        nab = place("nab", [P, NA_HEADS, 2, S_LAT], F32, A0 + 68 * K1)
        prob = place("prob", [P, 2, 2, T], F32, A0 + 76 * K1)
        probT = place("probT", [P, 2, 4, S_LAT], F32, A0 + 84 * K1)
        rp = place("rp", [P, 2, T], F32, A0 + 76 * K1)
        ft = place("ft", [P, 2, 512], F32, A0 + 80 * K1)
        fd = place("fd", [P, 2, P], F32, A0 + 84 * K1)
        u = place("u", [P, T // P, 256], F32, A0 + 85 * K1)
        fpq = place("fpq", [P, 512], F32, A0 + 89 * K1)
        tmp = place("tmp", [P, 2, T], F32, A0 + 68 * K1)
        m_hi = place("m_hi", [P, KB, T], F32R, A0 + 32 * K1)
        m_lo = place("m_lo", [P, KB, T], F32R, A0 + 48 * K1)
        g3 = place("g3", [P, 3, 2, T], F32, A0 + 76 * K1)
        gb = place("gb", [P, N_EXP, T], F32, A0)
        hid_hi = place("hid_hi", [P, 4, T], F32R, A0 + 32 * K1)
        hid_lo = place("hid_lo", [P, 4, T], F32R, A0 + 40 * K1)
        act_g = place("act_g", [P, 2, T], F32, A0 + 48 * K1)
        R0 = A0 + 56 * K1
        rt = place("rt", [P, 24, 4, N_EXP], F32, R0)
        gT = place("gT", [P, T], F32, A0 + 64 * K1)
        assert A0 + 92 * K1 <= nc.sbuf_usable_end, (A0, nc.sbuf_usable_end)

        o_sp = nc.alloc_sbuf_tensor_at("o_sp", [P, KB, 2, T], F32R, offset=A0)

        bank = [ctx.enter_context(nc.psum_tensor(f"bank{i}", [P, 512], F32)) for i in range(8)]

        def sem(name):
            return ctx.enter_context(nc.semaphore(name))

        full = [sem(f"bank_full{i}") for i in range(8)]
        free = [sem(f"bank_free{i}") for i in range(8)]
        raw_full = [sem(f"raw_full{i}") for i in range(RAW)]
        raw_free = [sem(f"raw_free{i}") for i in range(RAW)]
        hi_done = sem("hi_done")
        lo_done = sem("lo_done")
        chunk_used = sem("chunk_used")
        vec_in = sem("vec_in")
        x_in = sem("x_in")
        cst_in = [sem(f"cst_in{l}") for l in range(DEPTH)]
        nab_in = [sem(f"nab_in{l}") for l in range(DEPTH)]
        consts = sem("consts")
        cs_done = sem("cs_done")
        mod_done = [sem(f"mod_done{l}") for l in range(DEPTH)]
        rw_done = sem("rw_done")
        x_done = sem("x_done")
        sq_done = sem("sq_done")
        sq_used = sem("sq_used")
        root_done = sem("root_done")
        hf_done = sem("hf_done")
        hhi_done = sem("hhi_done")
        hlo_done = sem("hlo_done")
        chain = sem("chain")
        lat_done = sem("lat_done")
        latn_done = sem("latn_done")
        lathi_done = sem("lathi_done")
        latlo_done = sem("latlo_done")
        krope_done = sem("krope_done")
        kcopy_done = sem("kcopy_done")
        pe_terms = sem("pe_terms")
        q_done = sem("q_done")
        nab_done = sem("nab_done")
        qkv_act = sem("qkv_act")
        qkv_dve = sem("qkv_dve")
        fpq_done = sem("fpq_done")
        fpq_used = sem("fpq_used")
        ohi_done = sem("ohi_done")
        olo_done = sem("olo_done")
        max_done = sem("max_done")
        exp_done = sem("exp_done")
        prob_done = sem("prob_done")
        tr_done = sem("tr_done")
        pta_done = sem("pta_done")
        ptv_done = sem("ptv_done")
        pv_done = sem("pv_done")
        att_end = sem("att_end")
        sig_done = sem("sig_done")
        m_done = sem("m_done")
        mhi_done = sem("mhi_done")
        mlo_done = sem("mlo_done")
        merge_end = sem("merge_end")
        sc_done = sem("sc_done")
        gate_done = sem("gate_done")
        gT_done = sem("gT_done")
        gr_done = sem("gr_done")
        gb_in = [sem(f"gb_in{l}") for l in range(DEPTH)]
        silu_done = sem("silu_done")
        gated = sem("gated")
        hidf_done = sem("hidf_done")
        hidhi_done = sem("hidhi_done")
        hidlo_done = sem("hidlo_done")
        hid_used = sem("hid_used")
        moe_end = sem("moe_end")
        y_done = sem("y_done")
        y_out = sem("y_out")

        held = [0] * 8
        turn = [0]

        def results(n, banks=None):
            got = []
            for i in range(n):
                b = banks[i] if banks else turn[0] % 8
                if not banks:
                    turn[0] += 1
                got.append((b, held[b]))
                held[b] += 1
            return got

        def items(l):
            got = []
            for h in range(HEADS):
                got.append(("mla", h, 0, 0, T // P))
                if l == 0:
                    got.append(("mla", h, S_LAT, S_LAT, S_CTX // P))
            got.sort(key=lambda it: (it[1] // 2, it[2], it[1]))
            na = []
            for h in range(NA_HEADS):
                na.append(("na", h, 0, 0, T // P))
                if l == 0:
                    na.append(("na", h, S_LAT, S_LAT, S_CTX // P))
            na.sort(key=lambda it: (it[1] // 2, it[2], it[1]))
            return got + na

        N_PAIR = N_EXP // 2
        plan = []
        for l in range(DEPTH):
            s = {"ada": results(1)} if l == 0 else {}
            s["norm1"] = results(1)
            for name, n in (("qlat", 2), ("kvlat", 2), ("qss", 1), ("kvss", 1), ("naq", 2), ("nak", 2),
                            ("nav", 2), ("u", 2 if l == 0 else 1), ("qup", 8), ("kup", 4), ("vup", 4), ("ftp", 4 if l == 0 else 2)):
                s[name] = results(n)
            s["fto"] = results(len(s["ftp"]))
            its = items(l)
            s["S"] = [results(2, [2 * (i % 2), 2 * (i % 2) + 1]) for i in range(len(its))]
            s["PT"] = [results(nk // 2, [4, 5]) for _, _, _, _, nk in its]
            s["O"] = [results(1, [6 + i % 2])[0] for i in range(len(its) // 2)]
            s["items"] = its
            s["merge"] = [{"gate": results(6), "br": results(6)} for _ in range(N_MERGE)]
            s["out"] = [results(2) for _ in range(N_OUT)]
            s["norm2"] = results(1)
            s["logit"] = results(1)
            s["gateT"] = results(1)
            s["moe0"] = list(held)
            per = 3 if l == 0 else 2
            for b in range(8):
                held[b] += N_PAIR * (per if b == 0 else 2)
            plan.append(s)
        last_norm = results(1)

        first = {}
        n_chunk = 0
        n_split = 0
        for l in range(DEPTH):
            if l == 0:
                first["ada"] = n_chunk
                n_chunk += N_ADA
            first["in", l] = (n_chunk, n_split)
            n = N_IN + N_UP + 4 * N_MERGE + N_OUT
            n_chunk += n
            n_split += n
            first["moe", l] = (n_chunk, n_split)
            n_chunk += N_PAIR * (9 if l == 0 else 6)
            n_split += N_PAIR * 6
        ADA_LOOP = N_ADA // N_PAIR

        def raw_of(l, s):
            return first["in", l][0] + s - first["in", l][1]

        block = ctx.enter_context(nc.Block())

        @block.sync
        def _(sp):
            sp.dma_start(x[:], xin).then_inc(x_in, 16)

            def load(c):
                if c >= RAW:
                    sp.wait_ge(raw_free[c % RAW], c // RAW)
                sp.dma_start(raw[:, c % RAW, :], wts[c]).then_inc(raw_full[c % RAW], 16)

            for c in range(first["in", 0][0]):
                load(c)
            for l in range(DEPTH):
                for c in range(first["in", l][0], first["moe", l][0]):
                    load(c)
                c0 = first["moe", l][0]
                per = 9 if l == 0 else 6
                with sp.Fori(0, N_PAIR, 1) as i:
                    for j in range(per):
                        s = (c0 + j) % RAW
                        sp.wait_ge(raw_free[s], i * (per // RAW) + (c0 + j) // RAW)
                        sp.dma_start(raw[:, s, :], wts[bass.ds(c0 + j + i * per, 1)].rearrange("o p n -> (o p) n"))\
                          .then_inc(raw_full[s], 16)
            sp.wait_ge(y_done, 8)
            sp.dma_start(out, x[:, :, 0:S_LAT]).then_inc(y_out, 16)
            sp.wait_ge(y_out, 16)

        @block.gpsimd
        def _(pool):
            pool.dma_start(vec[:], vecs).then_inc(vec_in, 16)
            nc.gpsimd.memset(ident[:], 0.0).then_inc(consts, 1)
            nc.gpsimd.memset(ones[:], 1.0).then_inc(consts, 1)
            nc.gpsimd.memset(eps[:], EPS).then_inc(consts, 1)
            pool.wait_ge(consts, 1)
            nc.gpsimd.affine_select(out=ident[:], in_=ident[:], compare_op=ALU.not_equal, fill=1.0, base=0,
                                    pattern=[[-1, P]], channel_multiplier=1).then_inc(consts, 1)
            for l in range(DEPTH):
                nq = T if l == 0 else S_LAT
                if l > 0:
                    pool.wait_ge(moe_end, l)
                pool.dma_start(rp[:], rope).then_inc(cst_in[l], 16)
                pool.dma_start(ft[:], dft[:, 0:1024].rearrange("p (a n) -> p a n", a=2)).then_inc(cst_in[l], 16)
                pool.dma_start(fd[:], dft[:, 1024:1280].rearrange("p (a n) -> p a n", a=2)).then_inc(cst_in[l], 16)
                pool.wait_ge(krope_done, l + 1)
                nc.gpsimd.tensor_copy(k[64:96, 1:HEADS, :], k[64:96, 0:1, :].to_broadcast([32, HEADS - 1, T]))\
                  .then_inc(kcopy_done, 1)
                for g in range(2):
                    pool.wait_ge(pe_terms, 2 * l + g + 1)
                    for a in range(4):
                        ins = nc.gpsimd.tensor_tensor(q[64:96, 4 * g + a, 0:nq], tmp[32 * a:32 * a + 32, 0, 0:nq],
                                                      tmp[32 * a:32 * a + 32, 1, 0:nq], ALU.add)
                    ins.then_inc(q_done, 1)
                pool.wait_ge(q_done, 2 * l + 2)
                pool.dma_start(nab[:], biases[l]).then_inc(nab_in[l], 16)
                pool.wait_ge(gT_done, l + 1)
                pool.dma_start(gate_rows[l, :, 0:nq], gT[0:N_EXP, 0:nq]).then_inc(gr_done, 16)
                pool.wait_ge(gr_done, 16 * (l + 1))
                for a in range(4):
                    src = gate_rows[l, 4 * a:4 * a + 4, 0:nq].rearrange("(o e) t -> o e t", o=1)
                    pool.dma_start(gb[:, 4 * a:4 * a + 4, 0:nq], src.to_broadcast([P, 4, nq])).then_inc(gb_in[l], 16)

        @block.scalar
        def _(act):
            n_sq = [0]

            def high(l, s):
                c = raw_of(l, s)
                act.wait_ge(raw_full[c % RAW], 16 * (c // RAW + 1))
                if s >= SPL:
                    act.wait_ge(chunk_used, s - SPL + 1)
                nc.scalar.copy(w_hi[:, s % SPL, :], raw[:, c % RAW, :]).then_inc(hi_done, 1)

            def square(src):
                n = n_sq[0]
                if n >= 2:
                    act.wait_ge(sq_used, n - 1)
                nc.scalar.activation(sq[:, n % 2, 0:src.shape[-1]], src, ACT.Square).then_inc(sq_done, 1)
                n_sq[0] += 1

            def root(res, n, width):
                b, was = res
                act.wait_ge(full[b], was + 1)
                ins = nc.scalar.activation(rinv[:, 0:n], bank[b][:, 0:n], ACT.Sqrt, bias=eps[:], scale=1.0 / width)
                ins.then_inc(free[b], 1)
                return ins

            def norm(l, which, nt):
                act.wait_ge(x_done, 2 * l + which + 1)
                for kb in range(KB):
                    square(x[:, kb, 0:nt])
                res = plan[l]["norm1" if which == 0 else "norm2"][0] if l < DEPTH else last_norm[0]
                root(res, nt, D)
                if l == DEPTH:
                    return
                n0 = (2 * l + which) * KB
                for kb in range(KB):
                    act.wait_ge(hf_done, n0 + kb + 1)
                    nc.scalar.copy(h_hi[:, kb, 0:nt], tmp[:, kb % 2, 0:nt]).then_inc(hhi_done, 1)

            act.wait_ge(vec_in, 16)
            nc.scalar.activation(cs[:], vec[:, V_C:V_C + 2 * KB].rearrange("p (k s) -> p k s", s=2), ACT.Silu)\
              .then_inc(cs_done, 1)
            nc.scalar.copy(rw_hi[:], vec[:, V_RW:V_RW + KB * N_EXP].rearrange("p (k e) -> p k e", e=N_EXP))\
              .then_inc(rw_done, 1)
            act.wait_ge(consts, 4)
            for l in range(DEPTH):
                nq = T if l == 0 else S_LAT
                L = plan[l]
                s0 = first["in", l][1]
                lay = l * V_LAYER
                if l == 0:
                    high(l, s0)
                    high(l, s0 + 1)
                norm(l, 0, T)
                high(l, s0 + 2)
                for i, (b, was) in enumerate(L["qlat"]):
                    act.wait_ge(full[b], was + 1)
                    nc.scalar.copy(lat[:, i, 0:nq], bank[b][:, 0:nq]).then_inc(lat_done, 1)
                    square(bank[b][:, 0:nq])
                    act.wait_ge(sq_done, n_sq[0])
                    act.sem_inc(free[b], 1)
                high(l, s0 + 3)
                b, was = L["kvlat"][0]
                act.wait_ge(full[b], was + 1)
                nc.scalar.copy(lat[:, 2, :], bank[b][:]).then_inc(lat_done, 1)
                square(bank[b][:])
                act.wait_ge(sq_done, n_sq[0])
                act.sem_inc(free[b], 1)
                root(L["qss"][0], nq, Q_LORA)
                root2 = L["kvss"][0]
                act.wait_ge(latn_done, 3 * l + 2)
                root(root2, T, KV_LORA)
                for i in range(3):
                    n = nq if i < 2 else T
                    act.wait_ge(latn_done, 3 * l + i + 1)
                    nc.scalar.copy(lat_hi[:, i, 0:n], lat[:, i, 0:n]).then_inc(lathi_done, 1)
                high(l, s0 + 4)
                for i, (b, was) in enumerate(L["naq"]):
                    act.wait_ge(full[b], was + 1)
                    nc.scalar.copy(naq[:, i, 0:nq], bank[b][:, 0:nq]).then_inc(free[b], 1)
                high(l, s0 + 5)
                for i, (b, was) in enumerate(L["nak"]):
                    act.wait_ge(full[b], was + 1)
                    nc.scalar.copy(nak[:, i, :], bank[b][:]).then_inc(free[b], 1)
                high(l, s0 + 6)
                high(l, s0 + 7)
                high(l, s0 + 8)
                for i in (0, 2):
                    b, was = L["qup"][i]
                    act.wait_ge(full[b], was + 1)
                    nc.scalar.copy(q[0:64, 2 * i, 0:nq], bank[b][0:64, 0:nq])
                    nc.scalar.copy(q[0:64, 2 * i + 1, 0:nq], bank[b][64:128, 0:nq]).then_inc(free[b], 1)
                high(l, s0 + 9)
                for i in (0, 2):
                    b, was = L["kup"][i]
                    act.wait_ge(full[b], was + 1)
                    nc.scalar.copy(k[0:64, 2 * i, :], bank[b][0:64, :])
                    nc.scalar.copy(k[0:64, 2 * i + 1, :], bank[b][64:128, :]).then_inc(free[b], 1)
                for i in (0, 2):
                    b, was = L["vup"][i]
                    act.wait_ge(full[b], was + 1)
                    nc.scalar.copy(v[:, i, :], bank[b][:]).then_inc(free[b], 1)
                act.wait_ge(nab_in[l], 16)
                nc.scalar.mul(nab[:], nab[:], 1.0 / NA_SCALE).then_inc(nab_done, 1)
                for i, ((b, was), (b2, was2)) in enumerate(zip(L["ftp"], L["fto"])):
                    act.wait_ge(full[b], was + 1)
                    n = len(L["ftp"]) * l * 2 + i
                    prev = (4 if l else 0) + i
                    if prev:
                        act.wait_ge(fpq_used, prev)
                    nc.scalar.copy(fpq[:], bank[b][:]).then_inc(fpq_done, 1)
                    act.wait_ge(fpq_done, prev + 1)
                    act.sem_inc(free[b], 1)
                    act.wait_ge(full[b2], was2 + 1)
                    t0 = (i // 2) * S_LAT
                    nc.scalar.copy(o_sp[:, 6 + i % 2, 0, t0:t0 + S_LAT], bank[b2][:, 0:S_LAT]).then_inc(ohi_done, 1)
                its = L["items"]
                n0 = 0 if l == 0 else len(plan[0]["items"])
                o0 = 4 if l == 0 else 4 + len(plan[0]["items"]) // 2 + 2

                def softmax(i):
                    kind, h, q0, k0, nk = its[i]
                    scale = MLA_SCALE if kind == "mla" else NA_SCALE
                    act.wait_ge(max_done, n0 + i + 1)
                    if i >= 2:
                        act.wait_ge(tr_done, n0 + i - 1)
                    for qb in range(2):
                        b, was = L["S"][i][qb]
                        nc.scalar.activation(prob[:, i % 2, qb, 0:nk * P], bank[b][:, 0:nk * P], ACT.Exp,
                                             bias=smx[:, i % 2, 2 + qb:3 + qb], scale=scale,
                                             accum_out=smx[:, i % 2, 4 + qb:5 + qb]).then_inc(exp_done, 1)
                        act.wait_ge(exp_done, 2 * (n0 + i) + qb + 1)
                        act.sem_inc(free[b], 1)

                def turned(i):
                    b, was = L["PT"][i][0]
                    act.wait_ge(full[b], was + 1)
                    if i >= 2:
                        act.wait_ge(pv_done, n0 + i - 1)
                    nc.scalar.copy(probT[:, i % 2, 0:2, :], bank[b][:].rearrange("p (k q) -> p k q", k=2))\
                      .then_inc(pta_done, 1)
                    act.wait_ge(pta_done, n0 + i + 1)
                    act.sem_inc(free[b], 1)

                def out_high(i):
                    if i % 2 == 0:
                        return
                    kind, h, q0, k0, nk = its[i]
                    b, was = L["O"][i // 2]
                    act.wait_ge(full[b], was + 1)
                    ob = h // 2 + (0 if kind == "mla" else 4)
                    nc.scalar.copy(o_sp[:, ob, 0, q0:q0 + S_LAT], bank[b][:, 0:S_LAT]).then_inc(ohi_done, 1)

                for i in range(len(its) + 2):
                    if i < len(its):
                        softmax(i)
                    if 1 <= i <= len(its):
                        turned(i - 1)
                    if i >= 2:
                        out_high(i - 2)
                s = s0 + N_IN + N_UP
                for j in range(N_MERGE):
                    M = L["merge"][j]
                    for a in range(3):
                        if s + 2 < first["moe", l][1]:
                            high(l, s + 2)
                        s += 1
                        for c in range(2):
                            b, was = M["gate"][2 * a + c]
                            act.wait_ge(full[b], was + 1)
                            if j > 0:
                                act.wait_ge(mlo_done, 2 * (N_MERGE * l + j))
                            col = lay + V_BG + 8 * a + 2 * j + c
                            nc.scalar.activation(g3[:, a, c, 0:nq], bank[b][:, 0:nq], ACT.Sigmoid,
                                                 bias=vec[:, col:col + 1]).then_inc(sig_done, 1)
                            act.wait_ge(sig_done, 24 * l + 6 * j + 2 * a + c + 1)
                            act.sem_inc(free[b], 1)
                    high(l, s + 2)
                    s += 1
                    for c in range(2):
                        act.wait_ge(m_done, 2 * (N_MERGE * l + j) + c + 1)
                        nc.scalar.copy(m_hi[:, 2 * j + c, 0:nq], g3[:, 0, c, 0:nq]).then_inc(mhi_done, 1)
                for j in range(N_OUT):
                    if s + 2 < first["moe", l][1]:
                        high(l, s + 2)
                    s += 1
                norm(l, 1, nq)
                b, was = L["logit"][0]
                act.wait_ge(full[b], was + 1)
                nt = nq // P
                nc.scalar.activation(rt[:, 0, 0:nt, :], bank[b][:, 0:nt * N_EXP].rearrange("p (t e) -> p t e", e=N_EXP),
                                     ACT.Sigmoid).then_inc(sc_done, 1)
                act.wait_ge(sc_done, l + 1)
                act.sem_inc(free[b], 1)
                c0, s1 = first["moe", l]
                per = 9 if l == 0 else 6
                P0 = L["moe0"]
                with act.Fori(0, N_PAIR, 1) as i:
                    def high_in(j):
                        r = (c0 + j) % RAW
                        act.wait_ge(raw_full[r], i * (16 * per // RAW) + 16 * ((c0 + j) // RAW + 1))
                        act.wait_ge(chunk_used, i * 6 + s1 + j - SPL + 1)
                        nc.scalar.copy(w_hi[:, (s1 + j) % SPL, :], raw[:, r, :]).then_inc(hi_done, 1)
                    high_in(0)
                    high_in(1)
                    for e in range(2):
                        for c in range(2):
                            b = 4 * e + c
                            act.wait_ge(full[b], i * (3 if b == 0 and l == 0 else 2) + P0[b] + 1)
                            act.wait_ge(hidlo_done, i * 4 + 32 * l + 2 * e + 1)
                            nc.scalar.activation(act_g[:, c, 0:nq], bank[b][:, 0:nq], ACT.Silu).then_inc(silu_done, 1)
                            act.wait_ge(silu_done, i * 4 + 32 * l + 2 * e + c + 1)
                            act.sem_inc(free[b], 1)
                        high_in(2 + 2 * e)
                        if e == 0:
                            high_in(3)
                        for c in range(2):
                            act.wait_ge(hidf_done, i * 4 + 32 * l + 2 * e + c + 1)
                            act.wait_ge(hid_used, i + N_PAIR * l + 1)
                            nc.scalar.copy(hid_hi[:, 2 * e + c, 0:nq], act_g[:, c, 0:nq]).then_inc(hidhi_done, 1)
                    high_in(5)
                if l + 1 < DEPTH:
                    high(l + 1, first["in", l + 1][1])
                    high(l + 1, first["in", l + 1][1] + 1)
            norm(DEPTH, 0, S_LAT)

        @block.vector
        def _(dve):
            n_link = [0]

            def link(ins):
                n_link[0] += 1
                ins.then_inc(chain, 1)
                dve.wait_ge(chain, n_link[0])

            def low(l, s):
                c = raw_of(l, s)
                dve.wait_ge(hi_done, s + 1)
                nc.vector.tensor_tensor(w_lo[:, s % SPL, :], raw[:, c % RAW, :], w_hi[:, s % SPL, :].bitcast(F32),
                                        ALU.subtract).then_inc(lo_done, 1)
                dve.wait_ge(lo_done, s + 1)
                dve.sem_inc(raw_free[c % RAW], 1)

            def norm(l, which, nt):
                res = plan[l]["norm1" if which == 0 else "norm2"][0] if l < DEPTH else last_norm[0]
                b, was = res
                dve.wait_ge(free[b], was + 1)
                link(nc.vector.reciprocal(rinv[:, 0:nt], rinv[:, 0:nt]))
                n0 = (2 * l + which) * KB

                def scaled(kb):
                    link(nc.vector.tensor_tensor(tmp[:, kb % 2, 0:nt], x[:, kb, 0:nt], rinv[:, 0:nt], ALU.mult))
                    for st in range(nt // S_LAT):
                        c = slice(st * S_LAT, (st + 1) * S_LAT)
                        ins = nc.vector.tensor_scalar(tmp[:, kb % 2, c], tmp[:, kb % 2, c],
                                                      coef[:, l, which, kb, st:st + 1],
                                                      mod[:, l, 24 * which + kb, st:st + 1], ALU.mult, ALU.add)
                    ins.then_inc(hf_done, 1)

                def lower(kb):
                    dve.wait_ge(hhi_done, n0 + kb + 1)
                    nc.vector.tensor_tensor(h_lo[:, kb, 0:nt], tmp[:, kb % 2, 0:nt], h_hi[:, kb, 0:nt].bitcast(F32),
                                            ALU.subtract).then_inc(hlo_done, 1)
                    dve.wait_ge(hlo_done, n0 + kb + 1)

                for kb in range(KB + 1):
                    if kb < KB:
                        scaled(kb)
                    if kb >= 1:
                        lower(kb - 1)

            def modulation(l):
                lay = l * V_LAYER
                for which in range(2):
                    for st in range(2):
                        link(nc.vector.scalar_tensor_tensor(
                            out=coef[:, l, which, :, st], in0=mod[:, l, 24 * which + 8:24 * which + 16, st], scalar=1.0,
                            in1=vec[:, lay + V_N1 + 8 * which:lay + V_N1 + 8 * which + 8], op0=ALU.add, op1=ALU.mult))

            dve.sem_inc(hidlo_done, 1)
            dve.wait_ge(rw_done, 1)
            nc.vector.tensor_tensor(rw_lo[:], vec[:, V_RW:V_RW + KB * N_EXP].rearrange("p (k e) -> p k e", e=N_EXP),
                                    rw_hi[:].bitcast(F32), ALU.subtract).then_inc(rw_done, 1)
            b, was = plan[0]["ada"][0]
            dve.wait_ge(full[b], was + 1)
            link(nc.vector.tensor_tensor(mod[:, 0], bank[b][:, 0:2 * MOD].rearrange("p (m s) -> p m s", s=2),
                                         vec[:, V_BADA:V_BADA + MOD].rearrange("p (m o) -> p m o", o=1)
                                         .to_broadcast([P, MOD, 2]), ALU.add))
            dve.sem_inc(free[b], 1)
            dve.wait_ge(x_in, 16)
            dve.sem_inc(x_done, 1)
            for l in range(DEPTH):
                nq = T if l == 0 else S_LAT
                L = plan[l]
                s0 = first["in", l][1]
                lay = l * V_LAYER
                modulation(l)
                if l == 0:
                    low(l, s0)
                    low(l, s0 + 1)
                norm(l, 0, T)
                low(l, s0 + 2)
                low(l, s0 + 3)
                b, was = L["kvlat"][1]
                dve.wait_ge(full[b], was + 1)
                dve.wait_ge(cst_in[l], 48)
                nc.vector.tensor_tensor(tmp[0:32, 0, :], bank[b][0:32, :], rp[0:32, 0, :], ALU.mult)
                link(nc.vector.tensor_tensor(tmp[0:32, 1, :], bank[b][32:64, :], rp[32:64, 1, :], ALU.mult))
                dve.sem_inc(free[b], 1)
                nc.vector.tensor_tensor(k[64:96, 0, :], tmp[0:32, 0, :], tmp[0:32, 1, :], ALU.add)\
                  .then_inc(krope_done, 1)
                dve.wait_ge(krope_done, l + 1)
                b, was = L["qss"][0]
                dve.wait_ge(free[b], was + 1)
                link(nc.vector.reciprocal(rinv[:, 0:nq], rinv[:, 0:nq]))
                dve.wait_ge(lat_done, 3 * l + 3)
                for i in range(2):
                    nc.vector.scalar_tensor_tensor(out=lat[:, i, 0:nq], in0=lat[:, i, 0:nq],
                                                   scalar=vec[:, lay + V_QG + i:lay + V_QG + i + 1],
                                                   in1=rinv[:, 0:nq], op0=ALU.mult, op1=ALU.mult)\
                      .then_inc(latn_done, 1)
                b, was = L["kvss"][0]
                dve.wait_ge(free[b], was + 1)
                link(nc.vector.reciprocal(rinv[:], rinv[:]))
                nc.vector.scalar_tensor_tensor(out=lat[:, 2, :], in0=lat[:, 2, :],
                                               scalar=vec[:, lay + V_KVG:lay + V_KVG + 1],
                                               in1=rinv[:], op0=ALU.mult, op1=ALU.mult).then_inc(latn_done, 1)
                for i in range(3):
                    n = nq if i < 2 else T
                    dve.wait_ge(lathi_done, 3 * l + i + 1)
                    nc.vector.tensor_tensor(lat_lo[:, i, 0:n], lat[:, i, 0:n], lat_hi[:, i, 0:n].bitcast(F32),
                                            ALU.subtract).then_inc(latlo_done, 1)
                low(l, s0 + 4)
                low(l, s0 + 5)
                low(l, s0 + 6)
                for i, (b, was) in enumerate(L["nav"]):
                    dve.wait_ge(full[b], was + 1)
                    nc.vector.tensor_copy(nav[:, 2 * i:2 * i + 2, :], bank[b][:].rearrange("p (t n) -> p t n", t=2))\
                      .then_inc(free[b], 1)
                low(l, s0 + 7)
                for i, (b, was) in enumerate(L["u"]):
                    dve.wait_ge(full[b], was + 1)
                    nc.vector.tensor_copy(u[:, 2 * i:2 * i + 2, :], bank[b][:].rearrange("p (t n) -> p t n", t=2))\
                      .then_inc(free[b], 1)
                low(l, s0 + 8)
                for i in (1, 3):
                    b, was = L["qup"][i]
                    dve.wait_ge(full[b], was + 1)
                    nc.vector.tensor_copy(q[0:64, 2 * i, 0:nq], bank[b][0:64, 0:nq])
                    nc.vector.tensor_copy(q[0:64, 2 * i + 1, 0:nq], bank[b][64:128, 0:nq]).then_inc(free[b], 1)
                for g in range(2):
                    b, was = L["qup"][4 + g]
                    b2, was2 = L["qup"][6 + g]
                    dve.wait_ge(full[b], was + 1)
                    dve.wait_ge(full[b2], was2 + 1)
                    if g:
                        dve.wait_ge(q_done, 2 * l + g)
                    nc.vector.tensor_tensor(tmp[:, 0, 0:nq], bank[b][:, 0:nq], rp[:, 0, 0:nq], ALU.mult)\
                      .then_inc(free[b], 1)
                    nc.vector.tensor_tensor(tmp[:, 1, 0:nq], bank[b2][:, 0:nq], rp[:, 1, 0:nq], ALU.mult)\
                      .then_inc(pe_terms, 1)
                    dve.wait_ge(pe_terms, 2 * l + g + 1)
                    dve.sem_inc(free[b2], 1)
                low(l, s0 + 9)
                for i in (1, 3):
                    b, was = L["kup"][i]
                    dve.wait_ge(full[b], was + 1)
                    nc.vector.tensor_copy(k[0:64, 2 * i, :], bank[b][0:64, :])
                    nc.vector.tensor_copy(k[0:64, 2 * i + 1, :], bank[b][64:128, :]).then_inc(free[b], 1)
                for i in (1, 3):
                    b, was = L["vup"][i]
                    dve.wait_ge(full[b], was + 1)
                    nc.vector.tensor_copy(v[:, i, :], bank[b][:]).then_inc(free[b], 1)
                n_ft = 0 if l == 0 else 4
                o0 = 0 if l == 0 else 4 + len(plan[0]["items"]) // 2
                for i, (b2, was2) in enumerate(L["fto"]):
                    dve.wait_ge(ohi_done, o0 + i + 1)
                    t0 = (i // 2) * S_LAT
                    nc.vector.tensor_tensor(o_sp[:, 6 + i % 2, 1, t0:t0 + S_LAT], bank[b2][:, 0:S_LAT],
                                            o_sp[:, 6 + i % 2, 0, t0:t0 + S_LAT].bitcast(F32), ALU.subtract)\
                      .then_inc(free[b2], 1)
                o0 += len(L["fto"])
                its = L["items"]
                n0 = 0 if l == 0 else len(plan[0]["items"])

                def maxima(i):
                    kind, h, q0, k0, nk = its[i]
                    scale = MLA_SCALE if kind == "mla" else NA_SCALE
                    if i >= 2:
                        dve.wait_ge(exp_done, 2 * (n0 + i - 1))
                    for qb in range(2):
                        b, was = L["S"][i][qb]
                        dve.wait_ge(full[b], was + 1)
                        ins = nc.vector.tensor_reduce(smx[:, i % 2, qb:qb + 1], bank[b][:, 0:nk * P], AX, ALU.max)
                    link(ins)
                    nc.vector.tensor_scalar(smx[:, i % 2, 2:4], smx[:, i % 2, 0:2], -scale, None, ALU.mult)\
                      .then_inc(max_done, 1)

                def normalise(i):
                    kind, h, q0, k0, nk = its[i]
                    dve.wait_ge(exp_done, 2 * (n0 + i + 1))
                    link(nc.vector.reciprocal(smx[:, i % 2, 6:8], smx[:, i % 2, 4:6]))
                    for qb in range(2):
                        ins = nc.vector.tensor_scalar(prob[:, i % 2, qb, 0:nk * P], prob[:, i % 2, qb, 0:nk * P],
                                                      smx[:, i % 2, 6 + qb:7 + qb], None, ALU.mult)
                    ins.then_inc(prob_done, 1)

                def turned(i):
                    nk = its[i][4]
                    if nk < 4:
                        dve.wait_ge(pta_done, n0 + i + 1)
                        dve.sem_inc(ptv_done, 1)
                        return
                    b, was = L["PT"][i][1]
                    dve.wait_ge(full[b], was + 1)
                    if i >= 2:
                        dve.wait_ge(pv_done, n0 + i - 1)
                    nc.vector.tensor_copy(probT[:, i % 2, 2:4, :], bank[b][:].rearrange("p (k q) -> p k q", k=2))\
                      .then_inc(ptv_done, 1)
                    dve.wait_ge(ptv_done, n0 + i + 1)
                    dve.sem_inc(free[b], 1)

                def out_low(i):
                    if i % 2 == 0:
                        return
                    kind, h, q0, k0, nk = its[i]
                    b, was = L["O"][i // 2]
                    ob = h // 2 + (0 if kind == "mla" else 4)
                    dve.wait_ge(ohi_done, o0 + i // 2 + 1)
                    nc.vector.tensor_tensor(o_sp[:, ob, 1, q0:q0 + S_LAT], bank[b][:, 0:S_LAT],
                                            o_sp[:, ob, 0, q0:q0 + S_LAT].bitcast(F32), ALU.subtract)\
                      .then_inc(free[b], 1)

                for i in range(len(its) + 2):
                    if i < len(its):
                        maxima(i)
                    if 1 <= i <= len(its):
                        turned(i - 1)
                    if i < len(its):
                        normalise(i)
                    if i >= 2:
                        out_low(i - 2)
                s = s0 + N_IN + N_UP
                for j in range(N_MERGE):
                    M = L["merge"][j]
                    for a in range(4):
                        if s + 2 < first["moe", l][1]:
                            low(l, s + 2)
                        s += 1
                    for c in range(2):
                        dve.wait_ge(sig_done, 24 * l + 6 * j + 5 + c)
                        for a in range(3):
                            b, was = M["br"][3 * c + a]
                            dve.wait_ge(full[b], was + 1)
                            link(nc.vector.tensor_tensor(g3[:, a, c, 0:nq], g3[:, a, c, 0:nq], bank[b][:, 0:nq],
                                                         ALU.mult))
                            dve.sem_inc(free[b], 1)
                        link(nc.vector.tensor_tensor(g3[:, 0, c, 0:nq], g3[:, 0, c, 0:nq], g3[:, 1, c, 0:nq], ALU.add))
                        nc.vector.tensor_tensor(g3[:, 0, c, 0:nq], g3[:, 0, c, 0:nq], g3[:, 2, c, 0:nq], ALU.add)\
                          .then_inc(m_done, 1)
                    for c in range(2):
                        dve.wait_ge(mhi_done, 2 * (N_MERGE * l + j) + c + 1)
                        nc.vector.tensor_tensor(m_lo[:, 2 * j + c, 0:nq], g3[:, 0, c, 0:nq],
                                                m_hi[:, 2 * j + c, 0:nq].bitcast(F32), ALU.subtract)\
                          .then_inc(mlo_done, 1)
                for j in range(N_OUT):
                    if s + 2 < first["moe", l][1]:
                        low(l, s + 2)
                    s += 1
                    for c in range(2):
                        b, was = L["out"][j][c]
                        dve.wait_ge(full[b], was + 1)
                        for st in range(nq // S_LAT):
                            t = slice(st * S_LAT, (st + 1) * S_LAT)
                            ins = nc.vector.scalar_tensor_tensor(
                                out=x[:, 2 * j + c, t], in0=bank[b][:, t], scalar=mod[:, l, 16 + 2 * j + c, st:st + 1],
                                in1=x[:, 2 * j + c, t], op0=ALU.mult, op1=ALU.add)
                        ins.then_inc(free[b], 1)
                dve.wait_ge(free[b], was + 1)
                dve.sem_inc(x_done, 1)
                norm(l, 1, nq)
                nt = nq // P

                def R(i):
                    return rt[:, i, 0:nt, :]

                def G(i, a, n):
                    return rt[:, i, 0:nt, :].rearrange("p t (g e) -> p t g e", e=PER_GRP)[:, :, :, a:a + n]

                def H(i, a, n):
                    return rt[:, i, 0:nt, a:a + n]

                def tt(o, a, b_, op):
                    link(nc.vector.tensor_tensor(o, a, b_, op))

                dve.wait_ge(sc_done, l + 1)
                rb = vec[:, V_RB:V_RB + N_EXP].rearrange("p (o e) -> p o e", o=1).to_broadcast([P, nt, N_EXP])
                tt(R(1), R(0), rb, ALU.add)
                tt(G(2, 0, 2), G(1, 0, 2), G(1, 2, 2), ALU.max)
                tt(G(2, 2, 2), G(1, 0, 2), G(1, 2, 2), ALU.min)
                tt(G(3, 0, 1), G(2, 0, 1), G(2, 1, 1), ALU.max)
                tt(G(3, 1, 1), G(2, 0, 1), G(2, 1, 1), ALU.min)
                tt(G(3, 2, 1), G(2, 2, 1), G(2, 3, 1), ALU.max)
                tt(G(3, 1, 1), G(3, 1, 1), G(3, 2, 1), ALU.max)
                tt(H(4, 0, 4), G(3, 0, 1).rearrange("p t g o -> p t (g o)"),
                   G(3, 1, 1).rearrange("p t g o -> p t (g o)"), ALU.add)

                def beaten(o, i, view, n):
                    link(nc.vector.memset(o, 0.0))
                    for j in range(4):
                        if j > 0:
                            tt(view(6, 0, j), view(i, j, 1).to_broadcast(n + [j]), view(i, 0, j), ALU.is_gt)
                        if j < 3:
                            tt(view(6, j + 1, 3 - j), view(i, j, 1).to_broadcast(n + [3 - j]), view(i, j + 1, 3 - j),
                               ALU.is_ge)
                        if j > 0:
                            tt(view(5, 0, j), view(5, 0, j), view(6, 0, j), ALU.add)
                        if j < 3:
                            tt(view(5, j + 1, 3 - j), view(5, j + 1, 3 - j), view(6, j + 1, 3 - j), ALU.add)

                beaten(R(5), 4, H, [P, nt])
                link(nc.vector.tensor_scalar(H(7, 0, 4), H(5, 0, 4), 0.0, None, ALU.is_equal))
                beaten(R(5), 1, G, [P, nt, N_GRP])
                link(nc.vector.tensor_scalar(R(8), R(5), 1.5, None, ALU.is_le))
                tt(G(8, 0, 4), G(8, 0, 4), H(7, 0, 4).rearrange("p t (g o) -> p t g o", o=1)
                   .to_broadcast([P, nt, N_GRP, PER_GRP]), ALU.mult)
                tt(R(9), R(8), R(0), ALU.mult)
                link(nc.vector.tensor_reduce(H(10, 0, 1), R(9), AX, ALU.add))
                link(nc.vector.reciprocal(H(10, 1, 1), H(10, 0, 1)))
                nc.vector.tensor_tensor(R(11), R(9), H(10, 1, 1).to_broadcast([P, nt, N_EXP]), ALU.mult)\
                  .then_inc(gate_done, 1)
                b, was = L["gateT"][0]
                dve.wait_ge(full[b], was + 1)
                nc.vector.tensor_copy(gT[0:N_EXP, 0:nq], bank[b][0:N_EXP, 0:nq]).then_inc(gT_done, 1)
                dve.wait_ge(gT_done, l + 1)
                dve.sem_inc(free[b], 1)
                dve.wait_ge(gb_in[l], 64)
                c0, s1 = first["moe", l]
                per = 9 if l == 0 else 6
                P0 = L["moe0"]

                def uses(b):
                    return 3 if b == 0 and l == 0 else 2

                with dve.Fori(0, N_PAIR, 1) as i:
                    def low_in(j):
                        r = (c0 + j) % RAW
                        dve.wait_ge(hi_done, i * 6 + s1 + j + 1)
                        nc.vector.tensor_tensor(w_lo[:, (s1 + j) % SPL, :], raw[:, r, :],
                                                w_hi[:, (s1 + j) % SPL, :].bitcast(F32), ALU.subtract)\
                          .then_inc(lo_done, 1)
                        dve.wait_ge(lo_done, i * 6 + s1 + j + 1)
                        dve.sem_inc(raw_free[r], 1)
                    low_in(0)
                    low_in(1)
                    for e in range(2):
                        for c in range(2):
                            nb = 32 * l + 2 * e + c
                            dve.wait_ge(silu_done, i * 4 + nb + 1)
                            nc.vector.tensor_tensor(act_g[:, c, 0:nq], act_g[:, c, 0:nq],
                                                    gb[:, bass.ds(i * 2 + e, 1), 0:nq].rearrange("p o t -> p (o t)"),
                                                    ALU.mult).then_inc(gated, 1)
                            dve.wait_ge(gated, i * 4 + nb + 1)
                            b = 4 * e + 2 + c
                            dve.wait_ge(full[b], i * uses(b) + P0[b] + 1)
                            nc.vector.tensor_tensor(act_g[:, c, 0:nq], act_g[:, c, 0:nq], bank[b][:, 0:nq], ALU.mult)\
                              .then_inc(hidf_done, 1)
                            dve.wait_ge(hidf_done, i * 4 + nb + 1)
                            dve.sem_inc(free[b], 1)
                        low_in(2 + 2 * e)
                        if e == 0:
                            low_in(3)
                        for c in range(2):
                            nb = 32 * l + 2 * e + c
                            dve.wait_ge(hidhi_done, i * 4 + nb + 1)
                            nc.vector.tensor_tensor(hid_lo[:, 2 * e + c, 0:nq], act_g[:, c, 0:nq],
                                                    hid_hi[:, 2 * e + c, 0:nq].bitcast(F32), ALU.subtract)\
                              .then_inc(hidlo_done, 1)
                    low_in(5)
                    for b in range(8):
                        dve.wait_ge(full[b], i * uses(b) + P0[b] + 2)
                        for st in range(nq // S_LAT):
                            t = slice(st * S_LAT, (st + 1) * S_LAT)
                            ins = nc.vector.scalar_tensor_tensor(
                                out=x[:, b, t], in0=bank[b][:, t], scalar=mod[:, l, 40 + b, st:st + 1],
                                in1=x[:, b, t], op0=ALU.mult, op1=ALU.add)
                        ins.then_inc(free[b], 1)
                    if l == 0:
                        dve.wait_ge(full[0], i * 3 + P0[0] + 3)
                        nm = MOD // N_PAIR
                        nc.vector.tensor_tensor(
                            mod[:, 1, bass.ds(i * nm, nm), :], bank[0][:, 0:2 * nm].rearrange("p (m s) -> p m s", s=2),
                            vec[:, bass.ds(i * nm + V_LAYER + V_BADA, nm)].rearrange("p (m o) -> p m o", o=1)
                            .to_broadcast([P, nm, 2]), ALU.add).then_inc(free[0], 1)
                for b in range(8):
                    dve.wait_ge(free[b], P0[b] + N_PAIR * uses(b))
                dve.sem_inc(x_done, 1)
                dve.sem_inc(moe_end, 1)
                if l + 1 < DEPTH:
                    low(l + 1, first["in", l + 1][1])
                    low(l + 1, first["in", l + 1][1] + 1)
            b, was = last_norm[0]
            dve.wait_ge(free[b], was + 1)
            link(nc.vector.reciprocal(rinv[:, 0:S_LAT], rinv[:, 0:S_LAT]))
            for kb in range(KB):
                nc.vector.scalar_tensor_tensor(out=x[:, kb, 0:S_LAT], in0=x[:, kb, 0:S_LAT],
                                               scalar=vec[:, V_FN + kb:V_FN + kb + 1], in1=rinv[:, 0:S_LAT],
                                               op0=ALU.mult, op1=ALU.mult).then_inc(y_done, 1)

        @block.tensor
        def _(pe):
            n_sq = [0]

            def claim(res):
                b, was = res
                if was:
                    pe.wait_ge(free[b], was)

            def three(o, l_hi, l_lo, r_hi, r_lo, start, stop):
                nc.tensor.matmul(o, l_hi, r_hi, start=start, stop=False)
                nc.tensor.matmul(o, l_hi, r_lo, start=False, stop=False)
                return nc.tensor.matmul(o, l_lo, r_hi, start=False, stop=stop)

            def sums(res, n_blocks, nt):
                b, was = res
                claim(res)
                for i in range(n_blocks):
                    pe.wait_ge(sq_done, n_sq[0] + 1)
                    ins = nc.tensor.matmul(bank[b][:, 0:nt], ones[:], sq[:, n_sq[0] % 2, 0:nt], start=(i == 0),
                                           stop=(i == n_blocks - 1))
                    ins.then_inc(sq_used, 1)
                    n_sq[0] += 1
                pe.wait_ge(sq_used, n_sq[0])
                pe.sem_inc(full[b], 1)

            def wide(s, kb, col, n=P, width=CW):
                o = kb * width + col
                return w_hi[:, s % SPL, o:o + n], w_lo[:, s % SPL, o:o + n]

            def feature_major(s, results_, nt, used=True):
                for c, res in enumerate(results_):
                    b, was = res
                    claim(res)
                    for kb in range(KB):
                        wh, wl = wide(s, kb, c * P)
                        ins = three(bank[b][:, 0:nt], wh, wl, h_hi[:, kb, 0:nt], h_lo[:, kb, 0:nt], kb == 0, kb == KB - 1)
                    ins.then_inc(full[b], 1)
                pe.wait_ge(full[b], was + 1)
                pe.sem_inc(chunk_used, 1)

            def token_major(s, results_):
                for i, res in enumerate(results_):
                    b, was = res
                    claim(res)
                    for a in range(2):
                        t = slice((2 * i + a) * P, (2 * i + a + 1) * P)
                        for kb in range(KB):
                            wh, wl = wide(s, kb, 0, CW)
                            ins = three(bank[b][:, a * CW:(a + 1) * CW], h_hi[:, kb, t], h_lo[:, kb, t], wh, wl,
                                        kb == 0, kb == KB - 1)
                    ins.then_inc(full[b], 1)
                pe.wait_ge(full[b], was + 1)
                pe.sem_inc(chunk_used, 1)

            def ada(c, bk, col):
                for m in range(CW // P):
                    for kb in range(KB):
                        o = kb * CW + m * P
                        ins = nc.tensor.matmul(bank[bk][:, col + 2 * m:col + 2 * m + 2], raw[:, c, o:o + P], cs[:, kb, :],
                                               start=(kb == 0), stop=(kb == KB - 1))
                return ins

            pe.sem_inc(hid_used, 1)
            pe.wait_ge(consts, 4)
            pe.wait_ge(cs_done, 1)
            b, was = plan[0]["ada"][0]
            for c in range(N_ADA):
                pe.wait_ge(raw_full[c % RAW], 16 * (c // RAW + 1))
                ada(c % RAW, b, 4 * c).then_inc(raw_free[c % RAW], 1)
            pe.wait_ge(raw_free[(N_ADA - 1) % RAW], N_ADA // RAW)
            pe.sem_inc(full[b], 1)
            for l in range(DEPTH):
                nq = T if l == 0 else S_LAT
                L = plan[l]
                s0 = first["in", l][1]
                sums(L["norm1"][0], KB, T)
                pe.wait_ge(hlo_done, (2 * l + 1) * KB)
                pe.wait_ge(lo_done, s0 + 1)
                feature_major(s0, L["qlat"], nq)
                pe.wait_ge(lo_done, s0 + 2)
                feature_major(s0 + 1, L["kvlat"], T)
                sums(L["qss"][0], 2, nq)
                sums(L["kvss"][0], 1, T)
                pe.wait_ge(lo_done, s0 + 3)
                feature_major(s0 + 2, L["naq"], nq)
                pe.wait_ge(lo_done, s0 + 4)
                feature_major(s0 + 3, L["nak"], T)
                pe.wait_ge(lo_done, s0 + 5)
                token_major(s0 + 4, L["nav"])
                pe.wait_ge(lo_done, s0 + 6)
                token_major(s0 + 5, L["u"])
                pe.wait_ge(lo_done, s0 + 7)
                pe.wait_ge(latlo_done, 3 * l + 3)
                s = s0 + 6
                for i, res in enumerate(L["qup"]):
                    b, was = res
                    claim(res)
                    for kb in range(2):
                        wh, wl = wide(s, kb, i * P, P, 1024)
                        ins = three(bank[b][:, 0:nq], wh, wl, lat_hi[:, kb, 0:nq], lat_lo[:, kb, 0:nq], kb == 0, kb == 1)
                    ins.then_inc(full[b], 1)
                pe.wait_ge(full[b], was + 1)
                pe.sem_inc(chunk_used, 1)
                pe.wait_ge(lo_done, s0 + 8)
                s = s0 + 7
                for i, res in enumerate(L["kup"]):
                    b, was = res
                    claim(res)
                    wh, wl = wide(s, 0, i * P)
                    three(bank[b][:], wh, wl, lat_hi[:, 2, :], lat_lo[:, 2, :], True, True).then_inc(full[b], 1)
                for i, res in enumerate(L["vup"]):
                    b, was = res
                    claim(res)
                    wh, wl = wide(s, 0, 512, 512)
                    three(bank[b][:], lat_hi[:, 2, i * P:(i + 1) * P], lat_lo[:, 2, i * P:(i + 1) * P], wh, wl,
                          True, True).then_inc(full[b], 1)
                pe.wait_ge(full[b], was + 1)
                pe.sem_inc(chunk_used, 1)
                pe.wait_ge(cst_in[l], 48)
                for i, (res, res2) in enumerate(zip(L["ftp"], L["fto"])):
                    b, was = res
                    claim(res)
                    seq, fb = i // 2, i % 2
                    bu, wasu = L["u"][seq]
                    pe.wait_ge(free[bu], wasu + 1)
                    for a in range(2):
                        ins = nc.tensor.matmul(bank[b][:], u[:, 2 * seq + a, fb * P:(fb + 1) * P], ft[:, a, :],
                                               start=(a == 0), stop=(a == 1))
                    ins.then_inc(full[b], 1)
                    n = (4 if l else 0) + i
                    pe.wait_ge(fpq_done, n + 1)
                    b2, was2 = res2
                    claim(res2)
                    for a in range(2):
                        ins = nc.tensor.matmul(bank[b2][:, 0:S_LAT], fd[:, a, :], fpq[:, a * 256:(a + 1) * 256],
                                               start=(a == 0), stop=(a == 1))
                    ins.then_inc(full[b2], 1)
                    pe.wait_ge(full[b2], was2 + 1)
                    pe.sem_inc(fpq_used, 1)
                its = L["items"]
                n0 = 0 if l == 0 else len(plan[0]["items"])
                for name in ("naq", "nak", "nav", "qup", "kup", "vup"):
                    for b, was in L[name]:
                        pe.wait_ge(free[b], was + 1)
                pe.wait_ge(kcopy_done, l + 1)
                pe.wait_ge(q_done, 2 * l + 2)
                pe.wait_ge(nab_done, l + 1)

                def scores(i):
                    kind, h, q0, k0, nk = its[i]
                    for qb in range(2):
                        b, was = L["S"][i][qb]
                        claim((b, was))
                        t = slice(q0 + qb * P, q0 + (qb + 1) * P)
                        if kind == "mla":
                            ins = nc.tensor.matmul(bank[b][:, 0:nk * P], q[0:96, h, t], k[0:96, h, k0:k0 + nk * P],
                                                   start=True, stop=True)
                        else:
                            r = slice(64 * (h % 2), 64 * (h % 2) + 64)
                            ins = nc.tensor.matmul(bank[b][:, 0:nk * P], naq[r, h // 2, t],
                                                   nak[r, h // 2, k0:k0 + nk * P], start=True, stop=True)
                            if q0 == 0:
                                ins = nc.tensor.matmul(bank[b][:, 0:S_LAT], ident[:], nab[:, h, qb, :],
                                                       start=False, stop=True, skip_group_check=True)
                        ins.then_inc(full[b], 1)

                def turn_probs(i):
                    kind, h, q0, k0, nk = its[i]
                    pe.wait_ge(prob_done, n0 + i + 1)
                    for half in range(nk // 2):
                        b, was = L["PT"][i][half]
                        claim((b, was))
                        for a in range(2):
                            kb = 2 * half + a
                            for qb in range(2):
                                o = a * S_LAT + qb * P
                                ins = nc.tensor.transpose(bank[b][:, o:o + P], prob[:, i % 2, qb, kb * P:(kb + 1) * P],
                                                          ident[:])
                        ins.then_inc(full[b], 1)
                    pe.wait_ge(full[b], was + 1)
                    pe.sem_inc(tr_done, 1)

                def values(i):
                    kind, h, q0, k0, nk = its[i]
                    pe.wait_ge(pta_done, n0 + i + 1)
                    pe.wait_ge(ptv_done, n0 + i + 1)
                    b, was = L["O"][i // 2]
                    if i % 2 == 0:
                        claim((b, was))
                    r = 64 * (h % 2)
                    vv, w = (v, VD) if kind == "mla" else (nav, NA_D)
                    for kb in range(nk):
                        ins = nc.tensor.matmul(bank[b][r:r + 64, 0:S_LAT], vv[:, k0 // P + kb, h * w:(h + 1) * w],
                                               probT[:, i % 2, kb, :], start=(kb == 0), stop=(kb == nk - 1))
                    ins.then_inc(pv_done, 1)
                    if i % 2 == 1:
                        pe.wait_ge(pv_done, n0 + i + 1)
                        pe.sem_inc(full[b], 1)

                for i in range(-2, len(its)):
                    if i + 2 < len(its):
                        scores(i + 2)
                    if 0 <= i + 1 < len(its):
                        turn_probs(i + 1)
                    if i >= 0:
                        values(i)
                for b, was in L["fto"] + L["O"]:
                    pe.wait_ge(free[b], was + 1)
                s = s0 + N_IN + N_UP
                for j in range(N_MERGE):
                    M = L["merge"][j]
                    for a in range(3):
                        pe.wait_ge(lo_done, s + 1)
                        feature_major(s, M["gate"][2 * a:2 * a + 2], nq)
                        s += 1
                    pe.wait_ge(lo_done, s + 1)
                    for c in range(2):
                        for a, (k0, k1) in enumerate(((0, 4), (4, 6), (6, 8))):
                            b, was = M["br"][3 * c + a]
                            claim((b, was))
                            for kb in range(k0, k1):
                                wh, wl = wide(s, kb, c * P)
                                ins = three(bank[b][:, 0:nq], wh, wl, o_sp[:, kb, 0, 0:nq], o_sp[:, kb, 1, 0:nq],
                                            kb == k0, kb == k1 - 1)
                            ins.then_inc(full[b], 1)
                    pe.wait_ge(full[b], was + 1)
                    pe.sem_inc(chunk_used, 1)
                    s += 1
                pe.wait_ge(mlo_done, 8 * (l + 1))
                for j in range(N_OUT):
                    pe.wait_ge(lo_done, s + 1)
                    for c in range(2):
                        b, was = L["out"][j][c]
                        claim((b, was))
                        for kb in range(KB):
                            wh, wl = wide(s, kb, c * P)
                            ins = three(bank[b][:, 0:nq], wh, wl, m_hi[:, kb, 0:nq], m_lo[:, kb, 0:nq],
                                        kb == 0, kb == KB - 1)
                        ins.then_inc(full[b], 1)
                    pe.wait_ge(full[b], was + 1)
                    pe.sem_inc(chunk_used, 1)
                    s += 1
                sums(L["norm2"][0], KB, nq)
                pe.wait_ge(hlo_done, (2 * l + 2) * KB)
                pe.wait_ge(rw_done, 2)
                b, was = L["logit"][0]
                claim((b, was))
                for t in range(nq // P):
                    for kb in range(KB):
                        ins = three(bank[b][:, t * N_EXP:(t + 1) * N_EXP], h_hi[:, kb, t * P:(t + 1) * P],
                                    h_lo[:, kb, t * P:(t + 1) * P], rw_hi[:, kb, :], rw_lo[:, kb, :],
                                    kb == 0, kb == KB - 1)
                ins.then_inc(full[b], 1)
                b, was = L["gateT"][0]
                claim((b, was))
                pe.wait_ge(gate_done, l + 1)
                for t in range(nq // P):
                    ins = nc.tensor.transpose(bank[b][0:N_EXP, t * P:(t + 1) * P], rt[:, 11, t, :], ident[:])
                ins.then_inc(full[b], 1)
                c0, s1 = first["moe", l]
                per = 9 if l == 0 else 6
                P0 = L["moe0"]

                def uses(b):
                    return 3 if b == 0 and l == 0 else 2

                with pe.Fori(0, N_PAIR, 1) as i:
                    for e in range(2):
                        for w in range(2):
                            s = s1 + 2 * e + w
                            pe.wait_ge(lo_done, i * 6 + s + 1)
                            for c in range(2):
                                b = 4 * e + 2 * w + c
                                pe.wait_ge(free[b], i * uses(b) + P0[b])
                                for kb in range(KB):
                                    wh, wl = wide(s, kb, c * P)
                                    ins = three(bank[b][:, 0:nq], wh, wl, h_hi[:, kb, 0:nq], h_lo[:, kb, 0:nq],
                                                kb == 0, kb == KB - 1)
                                ins.then_inc(full[b], 1)
                            pe.wait_ge(full[b], i * uses(b) + P0[b] + 1)
                            pe.sem_inc(chunk_used, 1)
                    pe.wait_ge(lo_done, i * 6 + s1 + 6)
                    pe.wait_ge(hidlo_done, i * 4 + 32 * l + 5)
                    for b in range(8):
                        pe.wait_ge(free[b], i * uses(b) + P0[b] + 1)
                        for e in range(2):
                            for kb in range(2):
                                wh, wl = wide(s1 + 4 + e, kb, b * P, P, 1024)
                                ins = three(bank[b][:, 0:nq], wh, wl, hid_hi[:, 2 * e + kb, 0:nq],
                                            hid_lo[:, 2 * e + kb, 0:nq], e + kb == 0, e + kb == 2)
                        ins.then_inc(full[b], 1)
                    pe.wait_ge(full[7], i * 2 + P0[7] + 2)
                    pe.sem_inc(hid_used, 1)
                    pe.sem_inc(chunk_used, 2)
                    if l == 0:
                        pe.wait_ge(free[0], i * 3 + P0[0] + 2)
                        for j in range(ADA_LOOP):
                            r = (c0 + 6 + j) % RAW
                            pe.wait_ge(raw_full[r], i * (16 * per // RAW) + 16 * ((c0 + 6 + j) // RAW + 1))
                            ada(r, 0, 4 * j).then_inc(raw_free[r], 1)
                            last = (r, (c0 + 6 + j) // RAW + 1)
                        pe.wait_ge(raw_free[last[0]], i * (per // RAW) + last[1])
                        pe.sem_inc(full[0], 1)
            sums(last_norm[0], KB, S_LAT)


def _over_width(w):
    n = w.shape[1] // CW
    return w.reshape(KB, P, n, CW).transpose(2, 1, 0, 3).reshape(n, P, CH)


def _chunks(i):
    got = []
    for l in range(DEPTH):
        ada = _over_width(i["w_ada"][l])
        if l == 0:
            got.append(ada)
        w = i["w_in"][l]
        zeros = np.zeros((D, P - 2 * ROPE), np.float32)
        a = Q_LORA + KV_LORA
        rope = w[:, a:a + ROPE]
        swap = np.r_[ROPE // 2:ROPE, 0:ROPE // 2]
        got.append(_over_width(np.concatenate([w[:, :a], rope, rope[:, swap], zeros, w[:, a + ROPE:]], 1)))
        qu = i["w_q_up"][l].reshape(2, P, HEADS, NOPE + ROPE)
        pe = qu[..., NOPE:]
        qu = np.concatenate([qu[..., :NOPE].reshape(2, P, -1), pe.reshape(2, P, -1), pe[..., swap].reshape(2, P, -1)], 2)
        got.append(qu.transpose(1, 0, 2).reshape(1, P, CH))
        kv = i["w_kv_up"][l].reshape(KV_LORA, HEADS, NOPE + VD)
        kv = np.concatenate([kv[..., :NOPE].reshape(P, -1), kv[..., NOPE:].reshape(P, -1),
                             np.zeros((P, 1024), np.float32)], 1)
        got.append(kv.reshape(1, P, CH))
        gate = _over_width(i["w_gate"][l]).reshape(3, N_MERGE, P, CH)
        br = _over_width(np.concatenate([i["w_br_mla"][l], i["w_br_na"][l], i["w_br_ft"][l]], 0))
        for j in range(N_MERGE):
            got += [gate[:, j], br[j:j + 1]]
        got.append(_over_width(i["w_out"][l]))
        ada1 = _over_width(i["w_ada"][l + 1]) if l + 1 < DEPTH else None
        per = N_ADA // (N_EXP // 2)
        for e in range(0, N_EXP, 2):
            for f in (e, e + 1):
                got += [_over_width(i["w_e_gate"][l, f]), _over_width(i["w_e_up"][l, f])]
            for f in (e, e + 1):
                got.append(i["w_e_down"][l, f].reshape(2, P, D).transpose(1, 0, 2).reshape(1, P, CH))
            if ada1 is not None:
                got.append(ada1[per * (e // 2):per * (e // 2 + 1)])
    return np.concatenate(got, 0)


def _columns(vector):
    return vector.reshape(-1, P).T


def _vectors(i):
    cols = []
    for l in range(DEPTH):
        cols += [_columns(i[n][l]) for n in ("b_ada", "norm1_g", "norm2_g", "b_gate", "q_norm_g", "kv_norm_g")]
    cols.append(np.stack([_columns(i["c"][0]), _columns(i["c_ctx"])], 2).reshape(P, 2 * KB))
    cols.append(_columns(i["final_norm_g"]))
    cols.append(np.tile(i["router_bias"][None], (P, 1)))
    cols.append(i["router_w"].reshape(KB, P, N_EXP).transpose(1, 0, 2).reshape(P, -1))
    return np.concatenate(cols, 1)


def _rope_table():
    n = ROPE // 4
    inv = 10000.0 ** (-np.arange(n, dtype=np.float32) / n)
    t = np.arange(S_LAT)
    ang = np.concatenate([(t // GRID_W)[:, None] * inv, (t % GRID_W)[:, None] * inv], 1).astype(np.float32).T
    cos = np.concatenate([np.concatenate([np.cos(ang)] * 2, 0), np.ones((ROPE, S_CTX))], 1)
    sin = np.concatenate([np.concatenate([-np.sin(ang), np.sin(ang)], 0), np.zeros((ROPE, S_CTX))], 1)
    return np.stack([np.tile(cos, (4, 1)), np.tile(sin, (4, 1))], 1).astype(np.float32)


def _dft_tables():
    n = np.arange(S_LAT)
    ang = 2 * np.pi * (np.outer(n, n) % S_LAT) / S_LAT
    tok = np.concatenate([np.cos(ang), np.sin(ang)], 1).reshape(2, P, 2 * S_LAT).transpose(1, 0, 2).reshape(P, -1)
    f = np.arange(FT_D)
    ang = 2 * np.pi * (np.outer(f, f) % FT_D) / FT_D
    scale = 1.0 / np.sqrt(S_LAT * FT_D)
    pair = np.eye(P // FT_D)
    feat = [np.kron(pair, np.cos(ang)) * scale, -np.kron(pair, np.sin(ang)) * scale]
    return np.concatenate([tok] + feat, 1).astype(np.float32)


def _na_bias(rpb):
    t = np.arange(S_LAT)
    r, c = t // GRID_W, t % GRID_W
    rows = S_LAT // GRID_W
    start_r = np.clip(r - min(WIN_R, rows) // 2, 0, rows - min(WIN_R, rows))
    start_c = np.clip(c - WIN_C // 2, 0, GRID_W - WIN_C)
    seen = (r[None] >= start_r[:, None]) & (r[None] < start_r[:, None] + min(WIN_R, rows))
    seen &= (c[None] >= start_c[:, None]) & (c[None] < start_c[:, None] + WIN_C)
    dr = np.clip(r[None] - r[:, None] + WIN_R - 1, 0, 2 * WIN_R - 2)
    dc = np.clip(c[None] - c[:, None] + WIN_C - 1, 0, 2 * WIN_C - 2)
    full = np.where(seen, rpb[:, :, dr, dc], np.float32(NEG))
    return np.ascontiguousarray(full.reshape(DEPTH, NA_HEADS, 2, P, S_LAT).transpose(0, 3, 1, 2, 4))


def kernel(**inputs):
    import concourse.bacc as _bacc
    from concourse.bass_utils import run_bass_kernel_spmd as _run

    i = {n: np.asarray(a) for n, a in inputs.items()}
    tokens = np.concatenate([i["x"][0], i["ctx"][0]], 0)
    arrays = {
        "weights": _chunks(i),
        "tokens": np.ascontiguousarray(tokens.reshape(T, KB, P).transpose(2, 1, 0)),
        "vectors": np.ascontiguousarray(_vectors(i)),
        "rope": _rope_table(),
        "dft": _dft_tables(),
        "na_bias": _na_bias(i["na_rpb"]),
    }
    nc = _bacc.Bacc("TRN2", target_bir_lowering=False, num_devices=1)
    args = [nc.dram_tensor(n, a.shape, F32, kind="ExternalInput").ap() for n, a in arrays.items()]
    out = nc.dram_tensor("out", [P, KB, S_LAT], F32, kind="ExternalOutput").ap()
    gate_rows = nc.dram_tensor("gate_rows", [DEPTH, N_EXP, T], F32, kind="Internal").ap()
    build(nc, *args, out, gate_rows)
    r = _run(nc, [arrays], core_ids=[0])
    return np.asarray(r.results[0]["out"]).transpose(2, 1, 0).reshape(1, S_LAT, D)
```

```python
from contextlib import ExitStack

import concourse.bass as bass
from concourse import mybir
import numpy as np

F32 = mybir.dt.float32
F32R = mybir.dt.float32r
ALU = mybir.AluOpType
ACT = mybir.ActivationFunctionType
AX = mybir.AxisListType.X

P = 128
D = 1024
KB = D // P
S_LAT = 256
S_CTX = 256
T = S_LAT + S_CTX
DEPTH = 2
GRID_W = 64
HEADS, NOPE, ROPE, VD = 8, 64, 32, 64
Q_LORA, KV_LORA = 256, 128
NA_HEADS, NA_D = 4, 64
WIN_R, WIN_C = 8, 16
FT_G, FT_D = 4, 64
N_EXP, N_GRP = 16, 4
PER_GRP = N_EXP // N_GRP
FF = 256
EPS = 1e-6
NEG = -1e30
MLA_SCALE = (NOPE + ROPE) ** -0.5
NA_SCALE = NA_D ** -0.5
MOD = 6 * KB

CH = 2048
CW = 256
N_ADA = MOD * P // CW
N_IN = 6
N_UP = 2
N_MERGE = D // CW
N_OUT = D // CW
RAW = 3
EARLY_ADA = 2
SPL = 2

V_BADA, V_N1, V_N2, V_BG, V_QG, V_KVG = 0, 48, 56, 64, 88, 90
V_LAYER = 91
V_C = DEPTH * V_LAYER
V_FN = V_C + 2 * KB
V_RB = V_FN + KB
V_RW = V_RB + N_EXP
V_ALL = V_RW + KB * N_EXP


def build(nc, wts, xin, vecs, rope, dft, biases, out, gate_rows):
    ctx = ExitStack()
    with ctx:
        base = nc.sbuf_base + (-nc.sbuf_base) % 64
        at = [base]

        def place(name, shape, dt, off=None):
            size = 4 * int(np.prod(shape[1:]))
            o = at[0] if off is None else off
            if off is None:
                at[0] += size + (-size) % 32
            return nc.alloc_sbuf_tensor_at(name, shape, dt, offset=o)

        x = place("x", [P, KB, T], F32)
        h_hi = place("h_hi", [P, KB, T], F32R)
        h_lo = place("h_lo", [P, KB, T], F32R)
        raw = place("raw", [P, RAW, CH], F32)
        w_hi = place("w_hi", [P, SPL, CH], F32R)
        w_lo = place("w_lo", [P, SPL, CH], F32R)
        sq = place("sq", [P, 2, T], F32)
        rinv = place("rinv", [P, T], F32)
        vec = place("vec", [P, V_ALL], F32)
        ident = place("ident", [P, P], F32)
        ones = place("ones", [P, P], F32)
        eps = place("eps", [P, 1], F32)
        cs = place("cs", [P, KB, 2], F32)
        mod = place("mod", [P, DEPTH, MOD, 2], F32)
        coef = place("coef", [P, DEPTH, 2, KB, 2], F32)
        rw_hi = place("rw_hi", [P, KB, N_EXP], F32R)
        rw_lo = place("rw_lo", [P, KB, N_EXP], F32R)
        smx = place("smx", [P, 4, 8], F32)
        A0 = at[0]
        K1 = 1024
        q = place("q", [P, HEADS, T], F32, A0)
        lat_hi = place("lat_hi", [P, 3, T], F32R, A0 + 16 * K1)
        lat_lo = place("lat_lo", [P, 3, T], F32R, A0 + 22 * K1)
        k = place("k", [P, HEADS, T], F32, A0 + 32 * K1)
        v = place("v", [P, T // P, HEADS * VD], F32, A0 + 48 * K1)
        lat = place("lat", [P, 3, T], F32, A0 + 48 * K1)
        naq = place("naq", [P, 2, T], F32, A0 + 56 * K1)
        nak = place("nak", [P, 2, T], F32, A0 + 60 * K1)
        nav = place("nav", [P, T // P, 256], F32, A0 + 64 * K1)
        nab = place("nab", [P, NA_HEADS, 2, S_LAT], F32, A0 + 68 * K1)
        prob = place("prob", [P, 2, 2, T], F32, A0 + 76 * K1)
        probT = place("probT", [P, 2, 4, S_LAT], F32, A0 + 84 * K1)
        rp = place("rp", [P, 2, T], F32, A0 + 76 * K1)
        ft = place("ft", [P, 2, 512], F32, A0 + 80 * K1)
        fd = place("fd", [P, 2, P], F32, A0 + 84 * K1)
        u = place("u", [P, T // P, 256], F32, A0 + 85 * K1)
        fpq = place("fpq", [P, 512], F32, A0 + 89 * K1)
        tmp = place("tmp", [P, 2, T], F32, A0 + 68 * K1)
        mod_rows = place("mod_rows", [P, DEPTH, MOD * P], F32, A0)
        m_hi = place("m_hi", [P, KB, T], F32R, A0 + 32 * K1)
        m_lo = place("m_lo", [P, KB, T], F32R, A0 + 48 * K1)
        g3 = place("g3", [P, 3, 2, T], F32, A0 + 76 * K1)
        gb = place("gb", [P, N_EXP, T], F32, A0)
        hid_hi = place("hid_hi", [P, 4, T], F32R, A0 + 32 * K1)
        hid_lo = place("hid_lo", [P, 4, T], F32R, A0 + 40 * K1)
        act_g = place("act_g", [P, 2, T], F32, A0 + 48 * K1)
        R0 = A0 + 56 * K1
        rt = place("rt", [P, 24, 4, N_EXP], F32, R0)
        gT = place("gT", [P, T], F32, A0 + 64 * K1)
        assert A0 + 92 * K1 <= nc.sbuf_usable_end, (A0, nc.sbuf_usable_end)

        o_sp = nc.alloc_sbuf_tensor_at("o_sp", [P, KB, 2, T], F32R, offset=A0)

        bank = [ctx.enter_context(nc.psum_tensor(f"bank{i}", [P, 512], F32)) for i in range(8)]

        def sem(name):
            return ctx.enter_context(nc.semaphore(name))

        full = [sem(f"bank_full{i}") for i in range(8)]
        free = [sem(f"bank_free{i}") for i in range(8)]
        raw_full = [sem(f"raw_full{i}") for i in range(RAW)]
        hi_done = sem("hi_done")
        lo_done = sem("lo_done")
        vec_in = sem("vec_in")
        x_in = sem("x_in")
        cst_in = [sem(f"cst_in{l}") for l in range(DEPTH)]
        nab_in = [sem(f"nab_in{l}") for l in range(DEPTH)]
        consts = sem("consts")
        cs_done = sem("cs_done")
        rw_done = sem("rw_done")
        x_done = sem("x_done")
        sq_done = sem("sq_done")
        sq_used = sem("sq_used")
        hf_done = sem("hf_done")
        hhi_done = sem("hhi_done")
        hlo_done = sem("hlo_done")
        chain = sem("chain")
        lat_done = sem("lat_done")
        latn_done = sem("latn_done")
        lathi_done = sem("lathi_done")
        latlo_done = sem("latlo_done")
        krope_done = sem("krope_done")
        kcopy_done = sem("kcopy_done")
        pe_terms = sem("pe_terms")
        q_done = sem("q_done")
        nab_done = sem("nab_done")
        fpq_done = sem("fpq_done")
        fpq_used = sem("fpq_used")
        ohi_done = sem("ohi_done")
        olo_done = sem("olo_done")
        max_done = sem("max_done")
        exp_done = sem("exp_done")
        prob_done = sem("prob_done")
        pta_done = sem("pta_done")
        ptv_done = sem("ptv_done")
        pv_done = sem("pv_done")
        m_done = sem("m_done")
        mhi_done = sem("mhi_done")
        mlo_done = sem("mlo_done")
        sc_done = sem("sc_done")
        gate_done = sem("gate_done")
        gT_done = sem("gT_done")
        gr_done = sem("gr_done")
        gb_in = [sem(f"gb_in{l}") for l in range(DEPTH)]
        gb_first = [sem(f"gb_first{l}") for l in range(DEPTH)]
        hidf_done = sem("hidf_done")
        hidhi_done = sem("hidhi_done")
        hidlo_done = sem("hidlo_done")
        moe_end = sem("moe_end")
        y_done = sem("y_done")
        y_out = sem("y_out")

        held = [0] * 8
        turn = [0]

        def results(n, banks=None):
            got = []
            for i in range(n):
                b = banks[i] if banks else turn[0] % 8
                if not banks:
                    turn[0] += 1
                got.append((b, held[b]))
                held[b] += 1
            return got

        def items(l):
            got = []
            for h in range(HEADS):
                got.append(("mla", h, 0, 0, T // P))
                if l == 0:
                    got.append(("mla", h, S_LAT, S_LAT, S_CTX // P))
            got.sort(key=lambda it: (it[1] // 2, it[2], it[1]))
            na = []
            for h in range(NA_HEADS):
                na.append(("na", h, 0, 0, T // P))
                if l == 0:
                    na.append(("na", h, S_LAT, S_LAT, S_CTX // P))
            na.sort(key=lambda it: (it[1] // 2, it[2], it[1]))
            return got + na

        norm0 = results(1)
        ada_res = [results(N_ADA + 1) for l in range(DEPTH)]
        plan = []
        for l in range(DEPTH):
            s = {"norm1": norm0 if l == 0 else results(1)}
            for name, n in (("qlat", 2), ("kvlat", 2), ("qss", 1), ("kvss", 1), ("naq", 2), ("nak", 2),
                            ("nav", 2), ("u", 2 if l == 0 else 1), ("qup", 8), ("kup", 4), ("vup", 4), ("ftp", 4 if l == 0 else 2)):
                s[name] = results(n)
            s["fto"] = results(len(s["ftp"]))
            its = items(l)
            s["S"] = [results(2, [2 * (i % 2), 2 * (i % 2) + 1]) for i in range(len(its))]
            s["PT"] = [results(nk // 2, [4, 5]) for _, _, _, _, nk in its]
            s["O"] = [results(1, [6 + i % 2])[0] for i in range(len(its) // 2)]
            s["items"] = its
            s["merge"] = [{"gate": results(6), "br": results(6)} for _ in range(N_MERGE)]
            s["out"] = [results(2) for _ in range(N_OUT)]
            s["norm2"] = results(1)
            s["logit"] = results(1, [4])
            s["gateT"] = results(1, [5])
            s["moe0"] = list(held)
            for b in range(8):
                held[b] += N_EXP if b < 4 else 2 * N_EXP
            plan.append(s)
        last_norm = results(1)

        first = {}
        n_chunk = DEPTH * N_ADA
        n_split = 0
        for l in range(DEPTH):
            first["in", l] = (n_chunk, n_split)
            n = N_IN + N_UP + 4 * N_MERGE + N_OUT
            first["moe", l] = (n_chunk + n, n_split + n)
            n_chunk += n + 3 * N_EXP
            n_split += n + 3 * N_EXP
        C0 = DEPTH * N_ADA
        N_LOOP = (N_EXP - 2) // 2

        last_use = {}
        for l in range(DEPTH):
            L, s = plan[l], first["in", l][1]
            ends = [L[n][-1] for n in ("qlat", "kvlat", "naq", "nak", "nav", "u", "qup", "vup")]
            for M in L["merge"]:
                ends += [M["gate"][1], M["gate"][3], M["gate"][5], M["br"][5]]
            ends += [res[1] for res in L["out"]]
            P0 = L["moe0"]
            s2 = first["moe", l][1]
            for j, (b, was) in enumerate(ends):
                last_use[s + j] = (b, was + 1)
            last_use[s2 + 3 * N_EXP - 2] = (7, P0[7] + 2 * (N_EXP - 1))
            last_use[s2 + 3 * N_EXP - 1] = (7, P0[7] + 2 * N_EXP)

        block = ctx.enter_context(nc.Block())

        @block.sync
        def _(sp):
            sp.dma_start(vec[:], vecs).then_inc(vec_in, 16)

            def load(c, i=0):
                if C0 > c - RAW >= 0:
                    b, was = ada_res[(c - RAW) // N_ADA][(c - RAW) % N_ADA]
                    sp.wait_ge(full[b], was + 1)
                elif c - RAW >= C0:
                    sp.wait_ge(lo_done, i * 6 + c - RAW - C0 + 1)
                src = wts[c] if isinstance(i, int) else wts[bass.ds(i * 6 + c, 1)].rearrange("o p n -> (o p) n")
                sp.dma_start(raw[:, c % RAW, :], src).then_inc(raw_full[c % RAW], 16)

            for c in range(C0):
                if c == EARLY_ADA:
                    sp.dma_start(x[:], xin).then_inc(x_in, 16)
                load(c)
            for l in range(DEPTH):
                c1 = first["moe", l][0]
                for c in range(first["in", l][0], c1 + 2):
                    load(c)
                with sp.Fori(0, N_LOOP, 1) as i:
                    for j in range(6):
                        load(c1 + 2 + j, i)
                for c in range(c1 + 2 + 6 * N_LOOP, c1 + 3 * N_EXP):
                    load(c)
            sp.wait_ge(y_done, 8)
            sp.dma_start(out, x[:, :, 0:S_LAT]).then_inc(y_out, 16)
            sp.wait_ge(y_out, 16)

        @block.gpsimd
        def _(pool):
            nc.gpsimd.memset(ident[:], 0.0).then_inc(consts, 1)
            nc.gpsimd.memset(ones[:], 1.0).then_inc(consts, 1)
            nc.gpsimd.memset(eps[:], EPS).then_inc(consts, 1)
            pool.wait_ge(consts, 1)
            nc.gpsimd.affine_select(out=ident[:], in_=ident[:], compare_op=ALU.not_equal, fill=1.0, base=0,
                                    pattern=[[-1, P]], channel_multiplier=1).then_inc(consts, 1)
            for l in range(DEPTH):
                nq = T if l == 0 else S_LAT
                if l > 0:
                    pool.wait_ge(moe_end, l)
                pool.dma_start(rp[:], rope).then_inc(cst_in[l], 16)
                pool.dma_start(ft[:], dft[:, 0:1024].rearrange("p (a n) -> p a n", a=2)).then_inc(cst_in[l], 16)
                pool.dma_start(fd[:], dft[:, 1024:1280].rearrange("p (a n) -> p a n", a=2)).then_inc(cst_in[l], 16)
                pool.wait_ge(krope_done, l + 1)
                nc.gpsimd.tensor_copy(k[64:96, 1:HEADS, :], k[64:96, 0:1, :].to_broadcast([32, HEADS - 1, T]))\
                  .then_inc(kcopy_done, 1)
                for g in range(2):
                    pool.wait_ge(pe_terms, 2 * l + g + 1)
                    for a in range(4):
                        ins = nc.gpsimd.tensor_tensor(q[64:96, 4 * g + a, 0:nq], tmp[32 * a:32 * a + 32, 0, 0:nq],
                                                      tmp[32 * a:32 * a + 32, 1, 0:nq], ALU.add)
                    ins.then_inc(q_done, 1)
                pool.wait_ge(q_done, 2 * l + 2)
                pool.dma_start(nab[:], biases[l]).then_inc(nab_in[l], 16)
                pool.wait_ge(gT_done, l + 1)
                pool.dma_start(gate_rows[l, :, 0:nq], gT[0:N_EXP, 0:nq]).then_inc(gr_done, 16)
                pool.wait_ge(gr_done, 16 * (l + 1))
                for a, n_row in ((0, 1), (1, 3), (4, 4), (8, 4), (12, 4)):
                    src = gate_rows[l, a:a + n_row, 0:nq].rearrange("(o e) t -> o e t", o=1)
                    pool.dma_start(gb[:, a:a + n_row, 0:nq], src.to_broadcast([P, n_row, nq]))\
                        .then_inc(gb_in[l] if a else gb_first[l], 16)

        @block.scalar
        def _(act):
            n_sq = [0]

            def high(s, use=None, i=0):
                c = C0 + s
                act.wait_ge(raw_full[c % RAW], i * 32 + 16 * (c // RAW + 1))
                if s >= SPL:
                    b, n = use or last_use[s - SPL]
                    act.wait_ge(full[b], n)
                nc.scalar.copy(w_hi[:, s % SPL, :], raw[:, c % RAW, :]).then_inc(hi_done, 1)

            def square(src):
                n = n_sq[0]
                if n >= 2:
                    act.wait_ge(sq_used, n - 1)
                nc.scalar.activation(sq[:, n % 2, 0:src.shape[-1]], src, ACT.Square).then_inc(sq_done, 1)
                n_sq[0] += 1

            def root(res, n, width):
                b, was = res
                act.wait_ge(full[b], was + 1)
                ins = nc.scalar.activation(rinv[:, 0:n], bank[b][:, 0:n], ACT.Sqrt, bias=eps[:], scale=1.0 / width)
                ins.then_inc(free[b], 1)
                return ins

            def norm(l, which, nt):
                act.wait_ge(x_done, 2 * l + which + 1)
                for kb in range(KB):
                    square(x[:, kb, 0:nt])
                res = plan[l]["norm1" if which == 0 else "norm2"][0] if l < DEPTH else last_norm[0]
                root(res, nt, D)
                if l < DEPTH and (l, which) != (0, 0):
                    copies(l, which, nt)

            def copies(l, which, nt):
                n0 = (2 * l + which) * KB
                for kb in range(KB):
                    act.wait_ge(hf_done, n0 + kb + 1)
                    for st in range(nt // S_LAT):
                        c = slice(st * S_LAT, (st + 1) * S_LAT)
                        ins = nc.scalar.activation(h_hi[:, kb, c], tmp[:, kb % 2, c], ACT.Identity,
                                                   bias=mod[:, l, 24 * which + kb, st:st + 1])
                    ins.then_inc(hhi_done, 1)

            act.wait_ge(vec_in, 16)
            nc.scalar.activation(cs[:], vec[:, V_C:V_C + 2 * KB].rearrange("p (k s) -> p k s", s=2), ACT.Silu)\
              .then_inc(cs_done, 1)
            nc.scalar.copy(rw_hi[:], vec[:, V_RW:V_RW + KB * N_EXP].rearrange("p (k e) -> p k e", e=N_EXP))\
              .then_inc(rw_done, 1)
            act.wait_ge(consts, 4)
            norm(0, 0, T)
            for l in range(DEPTH):
                for c in range(N_ADA):
                    b, was = ada_res[l][c]
                    act.wait_ge(full[b], was + 1)
                    nc.scalar.copy(mod_rows[0:2, l, c * CW:(c + 1) * CW], bank[b][0:2, 0:CW]).then_inc(free[b], 1)
                    if l == 1 and c == 5:
                        copies(0, 0, T)
            for l in range(DEPTH):
                nq = T if l == 0 else S_LAT
                L = plan[l]
                s0 = first["in", l][1]
                lay = l * V_LAYER
                if l == 0:
                    high(s0)
                    high(s0 + 1)
                else:
                    norm(l, 0, T)
                high(s0 + 2)
                for i, (b, was) in enumerate(L["qlat"]):
                    act.wait_ge(full[b], was + 1)
                    nc.scalar.copy(lat[:, i, 0:nq], bank[b][:, 0:nq]).then_inc(lat_done, 1)
                    square(bank[b][:, 0:nq])
                    act.wait_ge(sq_done, n_sq[0])
                    act.sem_inc(free[b], 1)
                high(s0 + 3)
                b, was = L["kvlat"][0]
                act.wait_ge(full[b], was + 1)
                nc.scalar.copy(lat[:, 2, :], bank[b][:]).then_inc(lat_done, 1)
                square(bank[b][:])
                act.wait_ge(sq_done, n_sq[0])
                act.sem_inc(free[b], 1)
                root(L["qss"][0], nq, Q_LORA)
                act.wait_ge(latn_done, 3 * l + 2)
                root(L["kvss"][0], T, KV_LORA)
                for i in range(3):
                    n = nq if i < 2 else T
                    act.wait_ge(latn_done, 3 * l + i + 1)
                    nc.scalar.copy(lat_hi[:, i, 0:n], lat[:, i, 0:n]).then_inc(lathi_done, 1)
                high(s0 + 4)
                for i, (b, was) in enumerate(L["naq"]):
                    act.wait_ge(full[b], was + 1)
                    nc.scalar.copy(naq[:, i, 0:nq], bank[b][:, 0:nq]).then_inc(free[b], 1)
                high(s0 + 5)
                for i, (b, was) in enumerate(L["nak"]):
                    act.wait_ge(full[b], was + 1)
                    nc.scalar.copy(nak[:, i, :], bank[b][:]).then_inc(free[b], 1)
                high(s0 + 6)
                high(s0 + 7)
                high(s0 + 8)
                for i in (0, 2):
                    b, was = L["qup"][i]
                    act.wait_ge(full[b], was + 1)
                    nc.scalar.copy(q[0:64, 2 * i, 0:nq], bank[b][0:64, 0:nq])
                    nc.scalar.copy(q[0:64, 2 * i + 1, 0:nq], bank[b][64:128, 0:nq]).then_inc(free[b], 1)
                high(s0 + 9)
                for i in (0, 2):
                    b, was = L["kup"][i]
                    act.wait_ge(full[b], was + 1)
                    nc.scalar.copy(k[0:64, 2 * i, :], bank[b][0:64, :])
                    nc.scalar.copy(k[0:64, 2 * i + 1, :], bank[b][64:128, :]).then_inc(free[b], 1)
                for i in (0, 2):
                    b, was = L["vup"][i]
                    act.wait_ge(full[b], was + 1)
                    nc.scalar.copy(v[:, i, :], bank[b][:]).then_inc(free[b], 1)
                act.wait_ge(nab_in[l], 16)
                nc.scalar.mul(nab[:], nab[:], 1.0 / NA_SCALE).then_inc(nab_done, 1)
                for i, ((b, was), (b2, was2)) in enumerate(zip(L["ftp"], L["fto"])):
                    act.wait_ge(full[b], was + 1)
                    n = len(L["ftp"]) * l * 2 + i
                    prev = (4 if l else 0) + i
                    if prev:
                        act.wait_ge(fpq_used, prev)
                    nc.scalar.copy(fpq[:], bank[b][:]).then_inc(fpq_done, 1)
                    act.wait_ge(fpq_done, prev + 1)
                    act.sem_inc(free[b], 1)
                    act.wait_ge(full[b2], was2 + 1)
                    t0 = (i // 2) * S_LAT
                    nc.scalar.copy(o_sp[:, 6 + i % 2, 0, t0:t0 + S_LAT], bank[b2][:, 0:S_LAT]).then_inc(ohi_done, 1)
                its = L["items"]
                n0 = 0 if l == 0 else len(plan[0]["items"])
                o0 = 4 if l == 0 else 4 + len(plan[0]["items"]) // 2 + 2

                def softmax(i):
                    kind, h, q0, k0, nk = its[i]
                    scale = MLA_SCALE if kind == "mla" else NA_SCALE
                    if i >= 2:
                        b, was = L["PT"][i - 2][-1]
                        act.wait_ge(full[b], was + 1)
                    for qb in range(2):
                        b, was = L["S"][i][qb]
                        act.wait_ge(max_done, 2 * (n0 + i) + qb + 1)
                        nc.scalar.activation(prob[:, i % 2, qb, 0:nk * P], bank[b][:, 0:nk * P], ACT.Exp,
                                             bias=smx[:, i % 2, 2 + qb:3 + qb], scale=scale,
                                             accum_out=smx[:, i % 2, 4 + qb:5 + qb]).then_inc(exp_done, 1)
                        act.wait_ge(exp_done, 2 * (n0 + i) + qb + 1)
                        act.sem_inc(free[b], 1)

                def turned(i):
                    b, was = L["PT"][i][0]
                    act.wait_ge(full[b], was + 1)
                    if i >= 2:
                        act.wait_ge(pv_done, n0 + i - 1)
                    nc.scalar.copy(probT[:, i % 2, 0:2, :], bank[b][:].rearrange("p (k q) -> p k q", k=2))\
                      .then_inc(pta_done, 1)
                    act.wait_ge(pta_done, n0 + i + 1)
                    act.sem_inc(free[b], 1)

                def out_high(i):
                    if i % 2 == 0:
                        return
                    kind, h, q0, k0, nk = its[i]
                    b, was = L["O"][i // 2]
                    act.wait_ge(full[b], was + 1)
                    ob = h // 2 + (0 if kind == "mla" else 4)
                    nc.scalar.copy(o_sp[:, ob, 0, q0:q0 + S_LAT], bank[b][:, 0:S_LAT]).then_inc(ohi_done, 1)

                for i in range(len(its) + 3):
                    if 2 <= i < len(its) + 2:
                        turned(i - 2)
                    if i < len(its):
                        softmax(i)
                    if i >= 3:
                        out_high(i - 3)
                s = s0 + N_IN + N_UP
                for j in range(N_MERGE):
                    M = L["merge"][j]
                    for a in range(3):
                        if s + 2 < first["moe", l][1]:
                            high(s + 2)
                        s += 1
                        for c in range(2):
                            b, was = M["gate"][2 * a + c]
                            act.wait_ge(full[b], was + 1)
                            if j > 0:
                                act.wait_ge(mlo_done, 2 * (N_MERGE * l + j))
                            col = lay + V_BG + 8 * a + 2 * j + c
                            nc.scalar.activation(g3[:, a, c, 0:nq], bank[b][:, 0:nq], ACT.Sigmoid,
                                                 bias=vec[:, col:col + 1]).then_inc(free[b], 1)
                    for c in range(2):
                        if c == 1:
                            high(s + 2)
                            s += 1
                        act.wait_ge(m_done, 2 * (N_MERGE * l + j) + c + 1)
                        nc.scalar.copy(m_hi[:, 2 * j + c, 0:nq], g3[:, 0, c, 0:nq]).then_inc(mhi_done, 1)
                for j in range(N_OUT):
                    high(s + 2)
                    s += 1
                norm(l, 1, nq)
                c1, s1 = first["moe", l]
                P0 = L["moe0"]
                b, was = L["logit"][0]
                act.wait_ge(full[b], was + 1)
                nt = nq // P
                nc.scalar.activation(rt[:, 0, 0:nt, :], bank[b][:, 0:nt * N_EXP].rearrange("p (t e) -> p t e", e=N_EXP),
                                     ACT.Sigmoid).then_inc(sc_done, 1)
                act.wait_ge(sc_done, l + 1)
                act.sem_inc(free[b], 1)
                def silus(e):
                    for c in range(2):
                        act.wait_ge(full[c], P0[c] + 1 + e)
                        act.wait_ge(hidlo_done, 32 * l + 2 * e + 1)
                        nc.scalar.activation(act_g[:, c, 0:nq], bank[c][:, 0:nq], ACT.Silu).then_inc(free[c], 1)

                def hid_highs(e, par):
                    for c in range(2):
                        act.wait_ge(hidf_done, 32 * l + 2 * e + c + 1)
                        nc.scalar.copy(hid_hi[:, 2 * par + c, 0:nq], act_g[:, c, 0:nq]).then_inc(hidhi_done, 1)

                def step(e0, i, last=False):
                    e = e0 + 2 * i
                    s = s1 + 2 + 3 * (e0 - 1)
                    high(s + 2, (1, P0[1] + 1 + e), i)
                    silus(e)
                    high(s + 3, (3, P0[3] + 1 + e), i)
                    hid_highs(e, e0 % 2)
                    if not last:
                        high(s + 4, (7, P0[7] + 2 * e), i)

                silus(0)
                high(s1 + 2, (1, P0[1] + 1))
                high(s1 + 3, (3, P0[3] + 1))
                hid_highs(0, 0)
                with act.Fori(0, N_LOOP, 1) as i:
                    step(1, i)
                    step(2, i)
                step(N_EXP - 1, 0, last=(l + 1 == DEPTH))
                if l + 1 < DEPTH:
                    high(s1 + 3 * N_EXP + 1)
            norm(DEPTH, 0, S_LAT)

        @block.vector
        def _(dve):
            n_link = [0]

            def link(ins):
                n_link[0] += 1
                ins.then_inc(chain, 1)
                dve.wait_ge(chain, n_link[0])

            def low(s, i=0):
                c = C0 + s
                dve.wait_ge(hi_done, i * 6 + s + 1)
                nc.vector.tensor_tensor(w_lo[:, s % SPL, :], raw[:, c % RAW, :], w_hi[:, s % SPL, :].bitcast(F32),
                                        ALU.subtract).then_inc(lo_done, 1)

            def norm(l, which, nt):
                res = plan[l]["norm1" if which == 0 else "norm2"][0] if l < DEPTH else last_norm[0]
                b, was = res
                dve.wait_ge(free[b], was + 1)
                link(nc.vector.reciprocal(rinv[:, 0:nt], rinv[:, 0:nt]))
                n0 = (2 * l + which) * KB

                def scaled(kb):
                    if kb >= 2:
                        dve.wait_ge(hlo_done, n0 + kb - 1)
                    for st in range(nt // S_LAT):
                        c = slice(st * S_LAT, (st + 1) * S_LAT)
                        ins = nc.vector.scalar_tensor_tensor(
                            out=tmp[:, kb % 2, c], in0=x[:, kb, c], scalar=coef[:, l, which, kb, st:st + 1],
                            in1=rinv[:, c], op0=ALU.mult, op1=ALU.mult)
                    ins.then_inc(hf_done, 1)

                def lower(kb):
                    dve.wait_ge(hf_done, n0 + kb + 1)
                    dve.wait_ge(hhi_done, n0 + kb + 1)
                    for st in range(nt // S_LAT):
                        c = slice(st * S_LAT, (st + 1) * S_LAT)
                        ins = nc.vector.scalar_tensor_tensor(
                            out=h_lo[:, kb, c], in0=tmp[:, kb % 2, c], scalar=mod[:, l, 24 * which + kb, st:st + 1],
                            in1=h_hi[:, kb, c].bitcast(F32), op0=ALU.add, op1=ALU.subtract)
                    ins.then_inc(hlo_done, 1)

                scaled(0)
                scaled(1)
                for kb in range(KB):
                    lower(kb)
                    if kb + 2 < KB:
                        scaled(kb + 2)
                dve.wait_ge(hlo_done, n0 + KB)

            def modulation(l):
                lay = l * V_LAYER
                for which in range(2):
                    for st in range(2):
                        link(nc.vector.scalar_tensor_tensor(
                            out=coef[:, l, which, :, st], in0=mod[:, l, 24 * which + 8:24 * which + 16, st], scalar=1.0,
                            in1=vec[:, lay + V_N1 + 8 * which:lay + V_N1 + 8 * which + 8], op0=ALU.add, op1=ALU.mult))

            dve.sem_inc(hidlo_done, 1)
            dve.wait_ge(rw_done, 1)
            nc.vector.tensor_tensor(rw_lo[:], vec[:, V_RW:V_RW + KB * N_EXP].rearrange("p (k e) -> p k e", e=N_EXP),
                                    rw_hi[:].bitcast(F32), ALU.subtract).then_inc(rw_done, 1)
            dve.wait_ge(x_in, 16)
            dve.sem_inc(x_done, 1)
            for l in range(DEPTH):
                b, was = ada_res[l][N_ADA]
                dve.wait_ge(full[b], was + 1)
                o = l * V_LAYER + V_BADA
                nc.vector.tensor_tensor(mod[:, l], bank[b][:, 0:2 * MOD].rearrange("p (m s) -> p m s", s=2),
                                        vec[:, o:o + MOD].rearrange("p (m o) -> p m o", o=1)
                                        .to_broadcast([P, MOD, 2]), ALU.add).then_inc(free[b], 1)
                dve.wait_ge(free[b], was + 1)
                modulation(l)
                if l == 0:
                    norm(0, 0, T)
            for l in range(DEPTH):
                nq = T if l == 0 else S_LAT
                L = plan[l]
                s0 = first["in", l][1]
                lay = l * V_LAYER
                if l == 0:
                    low(s0)
                    low(s0 + 1)
                else:
                    norm(l, 0, T)
                low(s0 + 2)
                low(s0 + 3)
                b, was = L["kvlat"][1]
                dve.wait_ge(full[b], was + 1)
                dve.wait_ge(cst_in[l], 48)
                nc.vector.tensor_tensor(tmp[0:32, 0, :], bank[b][0:32, :], rp[0:32, 0, :], ALU.mult)
                link(nc.vector.tensor_tensor(tmp[0:32, 1, :], bank[b][32:64, :], rp[32:64, 1, :], ALU.mult))
                dve.sem_inc(free[b], 1)
                nc.vector.tensor_tensor(k[64:96, 0, :], tmp[0:32, 0, :], tmp[0:32, 1, :], ALU.add)\
                  .then_inc(krope_done, 1)
                dve.wait_ge(krope_done, l + 1)
                b, was = L["qss"][0]
                dve.wait_ge(free[b], was + 1)
                link(nc.vector.reciprocal(rinv[:, 0:nq], rinv[:, 0:nq]))
                dve.wait_ge(lat_done, 3 * l + 3)
                for i in range(2):
                    nc.vector.scalar_tensor_tensor(out=lat[:, i, 0:nq], in0=lat[:, i, 0:nq],
                                                   scalar=vec[:, lay + V_QG + i:lay + V_QG + i + 1],
                                                   in1=rinv[:, 0:nq], op0=ALU.mult, op1=ALU.mult)\
                      .then_inc(latn_done, 1)
                b, was = L["kvss"][0]
                dve.wait_ge(free[b], was + 1)
                link(nc.vector.reciprocal(rinv[:], rinv[:]))
                nc.vector.scalar_tensor_tensor(out=lat[:, 2, :], in0=lat[:, 2, :],
                                               scalar=vec[:, lay + V_KVG:lay + V_KVG + 1],
                                               in1=rinv[:], op0=ALU.mult, op1=ALU.mult).then_inc(latn_done, 1)
                for i in range(3):
                    n = nq if i < 2 else T
                    dve.wait_ge(lathi_done, 3 * l + i + 1)
                    nc.vector.tensor_tensor(lat_lo[:, i, 0:n], lat[:, i, 0:n], lat_hi[:, i, 0:n].bitcast(F32),
                                            ALU.subtract).then_inc(latlo_done, 1)
                low(s0 + 4)
                low(s0 + 5)
                low(s0 + 6)
                for i, (b, was) in enumerate(L["nav"]):
                    dve.wait_ge(full[b], was + 1)
                    nc.vector.tensor_copy(nav[:, 2 * i:2 * i + 2, :], bank[b][:].rearrange("p (t n) -> p t n", t=2))\
                      .then_inc(free[b], 1)
                low(s0 + 7)
                for i, (b, was) in enumerate(L["u"]):
                    dve.wait_ge(full[b], was + 1)
                    nc.vector.tensor_copy(u[:, 2 * i:2 * i + 2, :], bank[b][:].rearrange("p (t n) -> p t n", t=2))\
                      .then_inc(free[b], 1)
                low(s0 + 8)
                for i in (1, 3):
                    b, was = L["qup"][i]
                    dve.wait_ge(full[b], was + 1)
                    nc.vector.tensor_copy(q[0:64, 2 * i, 0:nq], bank[b][0:64, 0:nq])
                    nc.vector.tensor_copy(q[0:64, 2 * i + 1, 0:nq], bank[b][64:128, 0:nq]).then_inc(free[b], 1)
                for g in range(2):
                    b, was = L["qup"][4 + g]
                    b2, was2 = L["qup"][6 + g]
                    dve.wait_ge(full[b], was + 1)
                    dve.wait_ge(full[b2], was2 + 1)
                    if g:
                        dve.wait_ge(q_done, 2 * l + g)
                    nc.vector.tensor_tensor(tmp[:, 0, 0:nq], bank[b][:, 0:nq], rp[:, 0, 0:nq], ALU.mult)\
                      .then_inc(free[b], 1)
                    nc.vector.tensor_tensor(tmp[:, 1, 0:nq], bank[b2][:, 0:nq], rp[:, 1, 0:nq], ALU.mult)\
                      .then_inc(pe_terms, 1)
                    dve.wait_ge(pe_terms, 2 * l + g + 1)
                    dve.sem_inc(free[b2], 1)
                low(s0 + 9)
                for i in (1, 3):
                    b, was = L["kup"][i]
                    dve.wait_ge(full[b], was + 1)
                    nc.vector.tensor_copy(k[0:64, 2 * i, :], bank[b][0:64, :])
                    nc.vector.tensor_copy(k[0:64, 2 * i + 1, :], bank[b][64:128, :]).then_inc(free[b], 1)
                for i in (1, 3):
                    b, was = L["vup"][i]
                    dve.wait_ge(full[b], was + 1)
                    nc.vector.tensor_copy(v[:, i, :], bank[b][:]).then_inc(free[b], 1)
                n_ft = 0 if l == 0 else 4
                o0 = 0 if l == 0 else 4 + len(plan[0]["items"]) // 2
                for i, (b2, was2) in enumerate(L["fto"]):
                    dve.wait_ge(ohi_done, o0 + i + 1)
                    t0 = (i // 2) * S_LAT
                    nc.vector.tensor_tensor(o_sp[:, 6 + i % 2, 1, t0:t0 + S_LAT], bank[b2][:, 0:S_LAT],
                                            o_sp[:, 6 + i % 2, 0, t0:t0 + S_LAT].bitcast(F32), ALU.subtract)\
                      .then_inc(free[b2], 1)
                o0 += len(L["fto"])
                its = L["items"]
                n0 = 0 if l == 0 else len(plan[0]["items"])

                def maxima(i):
                    kind, h, q0, k0, nk = its[i]
                    scale = MLA_SCALE if kind == "mla" else NA_SCALE
                    if i >= 2:
                        dve.wait_ge(exp_done, 2 * (n0 + i - 1))
                    for qb in range(2):
                        b, was = L["S"][i][qb]
                        dve.wait_ge(full[b], was + 1)
                        link(nc.vector.tensor_reduce(smx[:, i % 2, qb:qb + 1], bank[b][:, 0:nk * P], AX, ALU.max))
                        nc.vector.tensor_scalar(smx[:, i % 2, 2 + qb:3 + qb], smx[:, i % 2, qb:qb + 1], -scale, None,
                                                ALU.mult).then_inc(max_done, 1)

                def normalise(i):
                    kind, h, q0, k0, nk = its[i]
                    for qb in range(2):
                        dve.wait_ge(exp_done, 2 * (n0 + i) + qb + 1)
                        link(nc.vector.reciprocal(smx[:, i % 2, 6 + qb:7 + qb], smx[:, i % 2, 4 + qb:5 + qb]))
                        ins = nc.vector.tensor_scalar(prob[:, i % 2, qb, 0:nk * P], prob[:, i % 2, qb, 0:nk * P],
                                                      smx[:, i % 2, 6 + qb:7 + qb], None, ALU.mult)
                    ins.then_inc(prob_done, 1)

                def turned(i):
                    nk = its[i][4]
                    if nk < 4:
                        dve.wait_ge(pta_done, n0 + i + 1)
                        dve.sem_inc(ptv_done, 1)
                        return
                    b, was = L["PT"][i][1]
                    dve.wait_ge(full[b], was + 1)
                    if i >= 2:
                        dve.wait_ge(pv_done, n0 + i - 1)
                    nc.vector.tensor_copy(probT[:, i % 2, 2:4, :], bank[b][:].rearrange("p (k q) -> p k q", k=2))\
                      .then_inc(ptv_done, 1)
                    dve.wait_ge(ptv_done, n0 + i + 1)
                    dve.sem_inc(free[b], 1)

                def out_low(i):
                    if i % 2 == 0:
                        return
                    kind, h, q0, k0, nk = its[i]
                    b, was = L["O"][i // 2]
                    ob = h // 2 + (0 if kind == "mla" else 4)
                    dve.wait_ge(ohi_done, o0 + i // 2 + 1)
                    nc.vector.tensor_tensor(o_sp[:, ob, 1, q0:q0 + S_LAT], bank[b][:, 0:S_LAT],
                                            o_sp[:, ob, 0, q0:q0 + S_LAT].bitcast(F32), ALU.subtract)\
                      .then_inc(free[b], 1)

                for i in range(len(its) + 3):
                    if 2 <= i < len(its) + 2:
                        turned(i - 2)
                    if 1 <= i <= len(its):
                        normalise(i - 1)
                    if i < len(its):
                        maxima(i)
                    if i >= 3:
                        out_low(i - 3)
                s = s0 + N_IN + N_UP
                for j in range(N_MERGE):
                    M = L["merge"][j]
                    for a in range(3):
                        low(s + 2)
                        s += 1
                    for c in range(2):
                        if c == 1:
                            low(s + 2)
                            s += 1
                        for a in range(3):
                            bg, wasg = M["gate"][2 * a + c]
                            dve.wait_ge(free[bg], wasg + 1)
                            b, was = M["br"][3 * c + a]
                            dve.wait_ge(full[b], was + 1)
                            link(nc.vector.tensor_tensor(g3[:, a, c, 0:nq], g3[:, a, c, 0:nq], bank[b][:, 0:nq],
                                                         ALU.mult))
                            dve.sem_inc(free[b], 1)
                        link(nc.vector.tensor_tensor(g3[:, 0, c, 0:nq], g3[:, 0, c, 0:nq], g3[:, 1, c, 0:nq], ALU.add))
                        nc.vector.tensor_tensor(g3[:, 0, c, 0:nq], g3[:, 0, c, 0:nq], g3[:, 2, c, 0:nq], ALU.add)\
                          .then_inc(m_done, 1)
                    for c in range(2):
                        dve.wait_ge(mhi_done, 2 * (N_MERGE * l + j) + c + 1)
                        nc.vector.tensor_tensor(m_lo[:, 2 * j + c, 0:nq], g3[:, 0, c, 0:nq],
                                                m_hi[:, 2 * j + c, 0:nq].bitcast(F32), ALU.subtract)\
                          .then_inc(mlo_done, 1)
                for j in range(N_OUT):
                    if j < N_OUT - 1:
                        low(s + 2)
                    s += 1
                    for c in range(2):
                        b, was = L["out"][j][c]
                        dve.wait_ge(full[b], was + 1)
                        for st in range(nq // S_LAT):
                            t = slice(st * S_LAT, (st + 1) * S_LAT)
                            ins = nc.vector.scalar_tensor_tensor(
                                out=x[:, 2 * j + c, t], in0=bank[b][:, t], scalar=mod[:, l, 16 + 2 * j + c, st:st + 1],
                                in1=x[:, 2 * j + c, t], op0=ALU.mult, op1=ALU.add)
                        ins.then_inc(free[b], 1)
                dve.wait_ge(free[b], was + 1)
                dve.sem_inc(x_done, 1)
                low(s + 1)
                norm(l, 1, nq)
                s1 = first["moe", l][1]
                nt = nq // P

                def R(i):
                    return rt[:, i, 0:nt, :]

                def G(i, a, n):
                    return rt[:, i, 0:nt, :].rearrange("p t (g e) -> p t g e", e=PER_GRP)[:, :, :, a:a + n]

                def H(i, a, n):
                    return rt[:, i, 0:nt, a:a + n]

                def tt(o, a, b_, op):
                    link(nc.vector.tensor_tensor(o, a, b_, op))

                dve.wait_ge(sc_done, l + 1)
                rb = vec[:, V_RB:V_RB + N_EXP].rearrange("p (o e) -> p o e", o=1).to_broadcast([P, nt, N_EXP])
                tt(R(1), R(0), rb, ALU.add)
                tt(G(2, 0, 2), G(1, 0, 2), G(1, 2, 2), ALU.max)
                tt(G(2, 2, 2), G(1, 0, 2), G(1, 2, 2), ALU.min)
                tt(G(3, 0, 1), G(2, 0, 1), G(2, 1, 1), ALU.max)
                tt(G(3, 1, 1), G(2, 0, 1), G(2, 1, 1), ALU.min)
                tt(G(3, 2, 1), G(2, 2, 1), G(2, 3, 1), ALU.max)
                tt(G(3, 1, 1), G(3, 1, 1), G(3, 2, 1), ALU.max)
                tt(H(4, 0, 4), G(3, 0, 1).rearrange("p t g o -> p t (g o)"),
                   G(3, 1, 1).rearrange("p t g o -> p t (g o)"), ALU.add)

                def beaten(o, i, view, n):
                    link(nc.vector.memset(o, 0.0))
                    for j in range(4):
                        if j > 0:
                            tt(view(6, 0, j), view(i, j, 1).to_broadcast(n + [j]), view(i, 0, j), ALU.is_gt)
                        if j < 3:
                            tt(view(6, j + 1, 3 - j), view(i, j, 1).to_broadcast(n + [3 - j]), view(i, j + 1, 3 - j),
                               ALU.is_ge)
                        if j > 0:
                            tt(view(5, 0, j), view(5, 0, j), view(6, 0, j), ALU.add)
                        if j < 3:
                            tt(view(5, j + 1, 3 - j), view(5, j + 1, 3 - j), view(6, j + 1, 3 - j), ALU.add)

                beaten(R(5), 4, H, [P, nt])
                link(nc.vector.tensor_scalar(H(7, 0, 4), H(5, 0, 4), 0.0, None, ALU.is_equal))
                beaten(R(5), 1, G, [P, nt, N_GRP])
                link(nc.vector.tensor_scalar(R(8), R(5), 1.5, None, ALU.is_le))
                tt(G(8, 0, 4), G(8, 0, 4), H(7, 0, 4).rearrange("p t (g o) -> p t g o", o=1)
                   .to_broadcast([P, nt, N_GRP, PER_GRP]), ALU.mult)
                tt(R(9), R(8), R(0), ALU.mult)
                link(nc.vector.tensor_reduce(H(10, 0, 1), R(9), AX, ALU.add))
                link(nc.vector.reciprocal(H(10, 1, 1), H(10, 0, 1)))
                nc.vector.tensor_tensor(R(11), R(9), H(10, 1, 1).to_broadcast([P, nt, N_EXP]), ALU.mult)\
                  .then_inc(gate_done, 1)
                P0 = L["moe0"]

                def products(e):
                    for c in range(2):
                        dve.wait_ge(full[2 + c], P0[2 + c] + 1 + e)
                        dve.wait_ge(free[c], P0[c] + 1 + e)
                        nc.vector.tensor_tensor(act_g[:, c, 0:nq], act_g[:, c, 0:nq], bank[2 + c][:, 0:nq], ALU.mult)\
                          .then_inc(free[2 + c], 1)

                def gated(e):
                    for c in range(2):
                        dve.wait_ge(free[2 + c], P0[2 + c] + 1 + e)
                        row = gb[:, e, 0:nq] if isinstance(e, int) else \
                            gb[:, bass.ds(e, 1), 0:nq].rearrange("p o t -> p (o t)")
                        nc.vector.tensor_tensor(act_g[:, c, 0:nq], act_g[:, c, 0:nq], row, ALU.mult)\
                          .then_inc(hidf_done, 1)

                def hid_lows(e, par):
                    for c in range(2):
                        dve.wait_ge(hidhi_done, 32 * l + 2 * e + c + 1)
                        nc.vector.tensor_tensor(hid_lo[:, 2 * par + c, 0:nq], act_g[:, c, 0:nq],
                                                hid_hi[:, 2 * par + c, 0:nq].bitcast(F32), ALU.subtract)\
                          .then_inc(hidlo_done, 1)

                def onto_x(e, blocks):
                    for m in blocks:
                        b = 4 + m % 4
                        dve.wait_ge(full[b], P0[b] + 1 + m // 4 + 2 * e)
                        for st in range(nq // S_LAT):
                            t = slice(st * S_LAT, (st + 1) * S_LAT)
                            ins = nc.vector.scalar_tensor_tensor(
                                out=x[:, m, t], in0=bank[b][:, t], scalar=mod[:, l, 40 + m, st:st + 1],
                                in1=x[:, m, t], op0=ALU.mult, op1=ALU.add)
                        ins.then_inc(free[b], 1)

                def step(e0, i, last=False):
                    e = e0 + 2 * i
                    s = s1 + 2 + 3 * (e0 - 1)
                    low(s + 2, i)
                    products(e)
                    onto_x(e - 1, range(4))
                    low(s + 3, i)
                    dve.wait_ge(gb_in[l], 64)
                    gated(e)
                    hid_lows(e, e0 % 2)
                    onto_x(e - 1, range(4, 6))
                    if not last:
                        low(s + 4, i)
                    onto_x(e - 1, range(6, 8))

                low(s1 + 2)
                bt, wast = L["gateT"][0]
                dve.wait_ge(full[bt], wast + 1)
                nc.vector.tensor_copy(gT[0:N_EXP, 0:nq], bank[bt][0:N_EXP, 0:nq]).then_inc(gT_done, 1)
                dve.wait_ge(gT_done, l + 1)
                dve.sem_inc(free[bt], 1)
                products(0)
                low(s1 + 3)
                dve.wait_ge(gb_first[l], 16)
                gated(0)
                hid_lows(0, 0)
                with dve.Fori(0, N_LOOP, 1) as i:
                    step(1, i)
                    step(2, i)
                step(N_EXP - 1, 0, last=(l + 1 == DEPTH))
                onto_x(N_EXP - 1, range(8))
                for b in range(4, 8):
                    dve.wait_ge(free[b], P0[b] + 2 * N_EXP)
                dve.sem_inc(x_done, 1)
                dve.sem_inc(moe_end, 1)
                if l + 1 < DEPTH:
                    low(s1 + 3 * N_EXP + 1)
            b, was = last_norm[0]
            dve.wait_ge(free[b], was + 1)
            link(nc.vector.reciprocal(rinv[:, 0:S_LAT], rinv[:, 0:S_LAT]))
            for kb in range(KB):
                nc.vector.scalar_tensor_tensor(out=x[:, kb, 0:S_LAT], in0=x[:, kb, 0:S_LAT],
                                               scalar=vec[:, V_FN + kb:V_FN + kb + 1], in1=rinv[:, 0:S_LAT],
                                               op0=ALU.mult, op1=ALU.mult).then_inc(y_done, 1)

        @block.tensor
        def _(pe):
            n_sq = [0]

            def claim(res):
                b, was = res
                if was:
                    pe.wait_ge(free[b], was)

            def three(o, l_hi, l_lo, r_hi, r_lo, start, stop):
                nc.tensor.matmul(o, l_hi, r_hi, start=start, stop=False)
                nc.tensor.matmul(o, l_hi, r_lo, start=False, stop=False)
                return nc.tensor.matmul(o, l_lo, r_hi, start=False, stop=stop)

            def sums(res, n_blocks, nt):
                b, was = res
                claim(res)
                for i in range(n_blocks):
                    pe.wait_ge(sq_done, n_sq[0] + 1)
                    ins = nc.tensor.matmul(bank[b][:, 0:nt], ones[:], sq[:, n_sq[0] % 2, 0:nt], start=(i == 0),
                                           stop=(i == n_blocks - 1))
                    ins.then_inc(sq_used, 1)
                    n_sq[0] += 1
                pe.wait_ge(sq_used, n_sq[0])
                pe.sem_inc(full[b], 1)

            def wide(s, kb, col, n=P, width=CW):
                o = kb * width + col
                return w_hi[:, s % SPL, o:o + n], w_lo[:, s % SPL, o:o + n]

            def feature_major(s, results_, nt, h0=None):
                if h0 is not None:
                    for res in results_:
                        claim(res)
                    for kb in range(KB):
                        pe.wait_ge(hlo_done, h0 + kb + 1)
                        for c, (b, was) in enumerate(results_):
                            wh, wl = wide(s, kb, c * P)
                            ins = three(bank[b][:, 0:nt], wh, wl, h_hi[:, kb, 0:nt], h_lo[:, kb, 0:nt],
                                        kb == 0, kb == KB - 1)
                            if kb == KB - 1:
                                ins.then_inc(full[b], 1)
                    return
                for c, res in enumerate(results_):
                    b, was = res
                    claim(res)
                    for kb in range(KB):
                        wh, wl = wide(s, kb, c * P)
                        ins = three(bank[b][:, 0:nt], wh, wl, h_hi[:, kb, 0:nt], h_lo[:, kb, 0:nt], kb == 0, kb == KB - 1)
                    ins.then_inc(full[b], 1)

            def token_major(s, results_):
                for i, res in enumerate(results_):
                    b, was = res
                    claim(res)
                    for a in range(2):
                        t = slice((2 * i + a) * P, (2 * i + a + 1) * P)
                        for kb in range(KB):
                            wh, wl = wide(s, kb, 0, CW)
                            ins = three(bank[b][:, a * CW:(a + 1) * CW], h_hi[:, kb, t], h_lo[:, kb, t], wh, wl,
                                        kb == 0, kb == KB - 1)
                    ins.then_inc(full[b], 1)

            pe.wait_ge(consts, 4)
            pe.wait_ge(cs_done, 1)
            for l in range(DEPTH):
                for c in range(N_ADA):
                    r = l * N_ADA + c
                    if r == EARLY_ADA:
                        sums(plan[0]["norm1"][0], KB, T)
                    b, was = ada_res[l][c]
                    claim((b, was))
                    pe.wait_ge(raw_full[r % RAW], 16 * (r // RAW + 1))
                    for kb in range(KB):
                        ins = nc.tensor.matmul(bank[b][0:2, 0:CW], cs[:, kb, :], raw[:, r % RAW, kb * CW:(kb + 1) * CW],
                                               start=(kb == 0), stop=(kb == KB - 1))
                    ins.then_inc(full[b], 1)
                for b, was in ada_res[l][:N_ADA]:
                    pe.wait_ge(free[b], was + 1)
                b, was = ada_res[l][N_ADA]
                claim((b, was))
                for m in range(MOD):
                    ins = nc.tensor.transpose(bank[b][:, 2 * m:2 * m + 2], mod_rows[0:2, l, m * P:(m + 1) * P],
                                              ident[0:2, 0:2])
                ins.then_inc(full[b], 1)
            for l in range(DEPTH):
                nq = T if l == 0 else S_LAT
                L = plan[l]
                s0 = first["in", l][1]
                if l > 0:
                    sums(L["norm1"][0], KB, T)
                pe.wait_ge(lo_done, s0 + 1)
                feature_major(s0, L["qlat"], nq, 2 * l * KB)
                pe.wait_ge(lo_done, s0 + 2)
                feature_major(s0 + 1, L["kvlat"], T)
                sums(L["qss"][0], 2, nq)
                sums(L["kvss"][0], 1, T)
                pe.wait_ge(lo_done, s0 + 3)
                feature_major(s0 + 2, L["naq"], nq)
                pe.wait_ge(lo_done, s0 + 4)
                feature_major(s0 + 3, L["nak"], T)
                pe.wait_ge(lo_done, s0 + 5)
                token_major(s0 + 4, L["nav"])
                pe.wait_ge(lo_done, s0 + 6)
                token_major(s0 + 5, L["u"])
                pe.wait_ge(lo_done, s0 + 7)
                pe.wait_ge(latlo_done, 3 * l + 3)
                s = s0 + 6
                for i, res in enumerate(L["qup"]):
                    b, was = res
                    claim(res)
                    for kb in range(2):
                        wh, wl = wide(s, kb, i * P, P, 1024)
                        ins = three(bank[b][:, 0:nq], wh, wl, lat_hi[:, kb, 0:nq], lat_lo[:, kb, 0:nq], kb == 0, kb == 1)
                    ins.then_inc(full[b], 1)
                pe.wait_ge(lo_done, s0 + 8)
                s = s0 + 7
                for i, res in enumerate(L["kup"]):
                    b, was = res
                    claim(res)
                    wh, wl = wide(s, 0, i * P)
                    three(bank[b][:], wh, wl, lat_hi[:, 2, :], lat_lo[:, 2, :], True, True).then_inc(full[b], 1)
                for i, res in enumerate(L["vup"]):
                    b, was = res
                    claim(res)
                    wh, wl = wide(s, 0, 512, 512)
                    three(bank[b][:], lat_hi[:, 2, i * P:(i + 1) * P], lat_lo[:, 2, i * P:(i + 1) * P], wh, wl,
                          True, True).then_inc(full[b], 1)
                pe.wait_ge(cst_in[l], 48)
                for i, (res, res2) in enumerate(zip(L["ftp"], L["fto"])):
                    b, was = res
                    claim(res)
                    seq, fb = i // 2, i % 2
                    bu, wasu = L["u"][seq]
                    pe.wait_ge(free[bu], wasu + 1)
                    for a in range(2):
                        ins = nc.tensor.matmul(bank[b][:], u[:, 2 * seq + a, fb * P:(fb + 1) * P], ft[:, a, :],
                                               start=(a == 0), stop=(a == 1))
                    ins.then_inc(full[b], 1)
                    n = (4 if l else 0) + i
                    pe.wait_ge(fpq_done, n + 1)
                    b2, was2 = res2
                    claim(res2)
                    for a in range(2):
                        ins = nc.tensor.matmul(bank[b2][:, 0:S_LAT], fd[:, a, :], fpq[:, a * 256:(a + 1) * 256],
                                               start=(a == 0), stop=(a == 1))
                    ins.then_inc(full[b2], 1)
                    pe.wait_ge(full[b2], was2 + 1)
                    pe.sem_inc(fpq_used, 1)
                its = L["items"]
                n0 = 0 if l == 0 else len(plan[0]["items"])
                for name in ("naq", "nak", "nav", "qup", "kup", "vup"):
                    for b, was in L[name]:
                        pe.wait_ge(free[b], was + 1)
                pe.wait_ge(kcopy_done, l + 1)
                pe.wait_ge(q_done, 2 * l + 2)
                pe.wait_ge(nab_done, l + 1)

                def scores(i):
                    kind, h, q0, k0, nk = its[i]
                    for qb in range(2):
                        b, was = L["S"][i][qb]
                        claim((b, was))
                        t = slice(q0 + qb * P, q0 + (qb + 1) * P)
                        if kind == "mla":
                            ins = nc.tensor.matmul(bank[b][:, 0:nk * P], q[0:96, h, t], k[0:96, h, k0:k0 + nk * P],
                                                   start=True, stop=True)
                        else:
                            r = slice(64 * (h % 2), 64 * (h % 2) + 64)
                            ins = nc.tensor.matmul(bank[b][:, 0:nk * P], naq[r, h // 2, t],
                                                   nak[r, h // 2, k0:k0 + nk * P], start=True, stop=True)
                            if q0 == 0:
                                ins = nc.tensor.matmul(bank[b][:, 0:S_LAT], ident[:], nab[:, h, qb, :],
                                                       start=False, stop=True, skip_group_check=True)
                        ins.then_inc(full[b], 1)

                def turn_probs(i):
                    kind, h, q0, k0, nk = its[i]
                    pe.wait_ge(prob_done, n0 + i + 1)
                    for half in range(nk // 2):
                        b, was = L["PT"][i][half]
                        claim((b, was))
                        for a in range(2):
                            kb = 2 * half + a
                            for qb in range(2):
                                o = a * S_LAT + qb * P
                                ins = nc.tensor.transpose(bank[b][:, o:o + P], prob[:, i % 2, qb, kb * P:(kb + 1) * P],
                                                          ident[:])
                        ins.then_inc(full[b], 1)

                def values(i):
                    kind, h, q0, k0, nk = its[i]
                    pe.wait_ge(pta_done, n0 + i + 1)
                    pe.wait_ge(ptv_done, n0 + i + 1)
                    b, was = L["O"][i // 2]
                    if i % 2 == 0:
                        claim((b, was))
                    r = 64 * (h % 2)
                    vv, w = (v, VD) if kind == "mla" else (nav, NA_D)
                    for kb in range(nk):
                        ins = nc.tensor.matmul(bank[b][r:r + 64, 0:S_LAT], vv[:, k0 // P + kb, h * w:(h + 1) * w],
                                               probT[:, i % 2, kb, :], start=(kb == 0), stop=(kb == nk - 1))
                    ins.then_inc(pv_done, 1)
                    if i % 2 == 1:
                        pe.wait_ge(pv_done, n0 + i + 1)
                        pe.sem_inc(full[b], 1)

                for i in range(-2, len(its)):
                    if i + 2 < len(its):
                        scores(i + 2)
                    if 0 <= i + 1 < len(its):
                        turn_probs(i + 1)
                    if i >= 0:
                        values(i)
                for b, was in L["fto"] + L["O"]:
                    pe.wait_ge(free[b], was + 1)
                s = s0 + N_IN + N_UP
                for j in range(N_MERGE):
                    M = L["merge"][j]
                    for a in range(3):
                        pe.wait_ge(lo_done, s + 1)
                        feature_major(s, M["gate"][2 * a:2 * a + 2], nq)
                        s += 1
                    pe.wait_ge(lo_done, s + 1)
                    for c in range(2):
                        for a, (k0, k1) in enumerate(((0, 4), (4, 6), (6, 8))):
                            b, was = M["br"][3 * c + a]
                            claim((b, was))
                            for kb in range(k0, k1):
                                wh, wl = wide(s, kb, c * P)
                                ins = three(bank[b][:, 0:nq], wh, wl, o_sp[:, kb, 0, 0:nq], o_sp[:, kb, 1, 0:nq],
                                            kb == k0, kb == k1 - 1)
                            ins.then_inc(full[b], 1)
                    s += 1
                for j in range(N_OUT):
                    pe.wait_ge(lo_done, s + 1)
                    for res in L["out"][j]:
                        claim(res)
                    for k0, k1 in ((0, KB - 2), (KB - 2, KB)):
                        for c, (b, was) in enumerate(L["out"][j]):
                            for kb in range(k0, k1):
                                pe.wait_ge(mlo_done, 8 * l + kb + 1)
                                wh, wl = wide(s, kb, c * P)
                                ins = three(bank[b][:, 0:nq], wh, wl, m_hi[:, kb, 0:nq], m_lo[:, kb, 0:nq],
                                            kb == 0, kb == KB - 1)
                            if k1 == KB:
                                ins.then_inc(full[b], 1)
                    s += 1
                sums(L["norm2"][0], KB, nq)
                s1 = first["moe", l][1]
                P0 = L["moe0"]
                pe.wait_ge(lo_done, s1 + 1)
                feature_major(s1, [(0, P0[0]), (1, P0[1])], nq, (2 * l + 1) * KB)
                pe.wait_ge(rw_done, 2)
                b, was = L["logit"][0]
                claim((b, was))
                for t in range(nq // P):
                    for kb in range(KB):
                        ins = three(bank[b][:, t * N_EXP:(t + 1) * N_EXP], h_hi[:, kb, t * P:(t + 1) * P],
                                    h_lo[:, kb, t * P:(t + 1) * P], rw_hi[:, kb, :], rw_lo[:, kb, :],
                                    kb == 0, kb == KB - 1)
                ins.then_inc(full[b], 1)
                pe.wait_ge(lo_done, s1 + 2)
                feature_major(s1 + 1, [(2, P0[2]), (3, P0[3])], nq)
                b, was = L["gateT"][0]
                claim((b, was))
                pe.wait_ge(gate_done, l + 1)
                for t in range(nq // P):
                    ins = nc.tensor.transpose(bank[b][0:N_EXP, t * P:(t + 1) * P], rt[:, 11, t, :], ident[:])
                ins.then_inc(full[b], 1)
                def down(s, e, par, i=0):
                    pe.wait_ge(lo_done, i * 6 + s + 1)
                    pe.wait_ge(hidlo_done, 32 * l + 2 * e + 3)
                    for m in range(KB):
                        b = 4 + m % 4
                        pe.wait_ge(free[b], P0[b] + m // 4 + 2 * e)
                        for kb in range(2):
                            wh, wl = wide(s, kb, m * P, P, 1024)
                            ins = three(bank[b][:, 0:nq], wh, wl, hid_hi[:, 2 * par + kb, 0:nq],
                                        hid_lo[:, 2 * par + kb, 0:nq], kb == 0, kb == 1)
                        ins.then_inc(full[b], 1)

                def step(e0, i):
                    e = e0 + 2 * i
                    s = s1 + 2 + 3 * (e0 - 1)
                    for w in range(2):
                        pe.wait_ge(lo_done, i * 6 + s + w + 1)
                        for c in range(2):
                            b = 2 * w + c
                            pe.wait_ge(free[b], P0[b] + e)
                            for kb in range(KB):
                                wh, wl = wide(s + w, kb, c * P)
                                ins = three(bank[b][:, 0:nq], wh, wl, h_hi[:, kb, 0:nq], h_lo[:, kb, 0:nq],
                                            kb == 0, kb == KB - 1)
                            ins.then_inc(full[b], 1)
                    down(s + 2, e - 1, (e0 - 1) % 2, i)

                with pe.Fori(0, N_LOOP, 1) as i:
                    step(1, i)
                    step(2, i)
                step(N_EXP - 1, 0)
                down(s1 + 3 * N_EXP - 1, N_EXP - 1, (N_EXP - 1) % 2)
            sums(last_norm[0], KB, S_LAT)


def _over_width(w):
    n = w.shape[1] // CW
    return w.reshape(KB, P, n, CW).transpose(2, 1, 0, 3).reshape(n, P, CH)


def _chunks(i):
    got = [_over_width(i["w_ada"][l]) for l in range(DEPTH)]
    for l in range(DEPTH):
        w = i["w_in"][l]
        zeros = np.zeros((D, P - 2 * ROPE), np.float32)
        a = Q_LORA + KV_LORA
        rope = w[:, a:a + ROPE]
        swap = np.r_[ROPE // 2:ROPE, 0:ROPE // 2]
        got.append(_over_width(np.concatenate([w[:, :a], rope, rope[:, swap], zeros, w[:, a + ROPE:]], 1)))
        qu = i["w_q_up"][l].reshape(2, P, HEADS, NOPE + ROPE)
        pe = qu[..., NOPE:]
        qu = np.concatenate([qu[..., :NOPE].reshape(2, P, -1), pe.reshape(2, P, -1), pe[..., swap].reshape(2, P, -1)], 2)
        got.append(qu.transpose(1, 0, 2).reshape(1, P, CH))
        kv = i["w_kv_up"][l].reshape(KV_LORA, HEADS, NOPE + VD)
        kv = np.concatenate([kv[..., :NOPE].reshape(P, -1), kv[..., NOPE:].reshape(P, -1),
                             np.zeros((P, 1024), np.float32)], 1)
        got.append(kv.reshape(1, P, CH))
        gate = _over_width(i["w_gate"][l]).reshape(3, N_MERGE, P, CH)
        br = _over_width(np.concatenate([i["w_br_mla"][l], i["w_br_na"][l], i["w_br_ft"][l]], 0))
        for j in range(N_MERGE):
            got += [gate[:, j], br[j:j + 1]]
        got.append(_over_width(i["w_out"][l]))
        down = [i["w_e_down"][l, e].reshape(2, P, D).transpose(1, 0, 2).reshape(1, P, CH) for e in range(N_EXP)]
        for e in range(N_EXP):
            got += [_over_width(i["w_e_gate"][l, e]), _over_width(i["w_e_up"][l, e])]
            if e > 0:
                got.append(down[e - 1])
        got.append(down[-1])
    return np.concatenate(got, 0)


def _columns(vector):
    return vector.reshape(-1, P).T


def _vectors(i):
    cols = []
    for l in range(DEPTH):
        cols += [_columns(i[n][l]) for n in ("b_ada", "norm1_g", "norm2_g", "b_gate", "q_norm_g", "kv_norm_g")]
    cols.append(np.stack([_columns(i["c"][0]), _columns(i["c_ctx"])], 2).reshape(P, 2 * KB))
    cols.append(_columns(i["final_norm_g"]))
    cols.append(np.tile(i["router_bias"][None], (P, 1)))
    cols.append(i["router_w"].reshape(KB, P, N_EXP).transpose(1, 0, 2).reshape(P, -1))
    return np.concatenate(cols, 1)


def _rope_table():
    n = ROPE // 4
    inv = 10000.0 ** (-np.arange(n, dtype=np.float32) / n)
    t = np.arange(S_LAT)
    ang = np.concatenate([(t // GRID_W)[:, None] * inv, (t % GRID_W)[:, None] * inv], 1).astype(np.float32).T
    cos = np.concatenate([np.concatenate([np.cos(ang)] * 2, 0), np.ones((ROPE, S_CTX))], 1)
    sin = np.concatenate([np.concatenate([-np.sin(ang), np.sin(ang)], 0), np.zeros((ROPE, S_CTX))], 1)
    return np.stack([np.tile(cos, (4, 1)), np.tile(sin, (4, 1))], 1).astype(np.float32)


def _dft_tables():
    n = np.arange(S_LAT)
    ang = 2 * np.pi * (np.outer(n, n) % S_LAT) / S_LAT
    tok = np.concatenate([np.cos(ang), np.sin(ang)], 1).reshape(2, P, 2 * S_LAT).transpose(1, 0, 2).reshape(P, -1)
    f = np.arange(FT_D)
    ang = 2 * np.pi * (np.outer(f, f) % FT_D) / FT_D
    scale = 1.0 / np.sqrt(S_LAT * FT_D)
    pair = np.eye(P // FT_D)
    feat = [np.kron(pair, np.cos(ang)) * scale, -np.kron(pair, np.sin(ang)) * scale]
    return np.concatenate([tok] + feat, 1).astype(np.float32)


def _na_bias(rpb):
    t = np.arange(S_LAT)
    r, c = t // GRID_W, t % GRID_W
    rows = S_LAT // GRID_W
    start_r = np.clip(r - min(WIN_R, rows) // 2, 0, rows - min(WIN_R, rows))
    start_c = np.clip(c - WIN_C // 2, 0, GRID_W - WIN_C)
    seen = (r[None] >= start_r[:, None]) & (r[None] < start_r[:, None] + min(WIN_R, rows))
    seen &= (c[None] >= start_c[:, None]) & (c[None] < start_c[:, None] + WIN_C)
    dr = np.clip(r[None] - r[:, None] + WIN_R - 1, 0, 2 * WIN_R - 2)
    dc = np.clip(c[None] - c[:, None] + WIN_C - 1, 0, 2 * WIN_C - 2)
    full = np.where(seen, rpb[:, :, dr, dc], np.float32(NEG))
    return np.ascontiguousarray(full.reshape(DEPTH, NA_HEADS, 2, P, S_LAT).transpose(0, 3, 1, 2, 4))


def kernel(**inputs):
    import concourse.bacc as _bacc
    from concourse.bass_utils import run_bass_kernel_spmd as _run

    i = {n: np.asarray(a) for n, a in inputs.items()}
    tokens = np.concatenate([i["x"][0], i["ctx"][0]], 0)
    arrays = {
        "weights": _chunks(i),
        "tokens": np.ascontiguousarray(tokens.reshape(T, KB, P).transpose(2, 1, 0)),
        "vectors": np.ascontiguousarray(_vectors(i)),
        "rope": _rope_table(),
        "dft": _dft_tables(),
        "na_bias": _na_bias(i["na_rpb"]),
    }
    nc = _bacc.Bacc("TRN2", target_bir_lowering=False, num_devices=1)
    args = [nc.dram_tensor(n, a.shape, F32, kind="ExternalInput").ap() for n, a in arrays.items()]
    out = nc.dram_tensor("out", [P, KB, S_LAT], F32, kind="ExternalOutput").ap()
    gate_rows = nc.dram_tensor("gate_rows", [DEPTH, N_EXP, T], F32, kind="Internal").ap()
    build(nc, *args, out, gate_rows)
    r = _run(nc, [arrays], core_ids=[0])
    return np.asarray(r.results[0]["out"]).transpose(2, 1, 0).reshape(1, S_LAT, D)
```
